# Optimizing a Trainium2 kernel written in Bass

```python
import math
import jax, jax.numpy as jnp
from jax import lax
import numpy as np

D_MODEL = 1024
BATCH = 1
SEQ = 256
DEPTH = 1

GRID_W = 64
N_DIFF_HEADS = 4
DIFF_HEAD_DIM = 64
DIFF_V_DIM = 2 * DIFF_HEAD_DIM
ROPE_THETA = 500000.0
ROPE_DIM = DIFF_HEAD_DIM // 4
Q_BLOCK = 128
N_NA_HEADS = 8
NA_HEAD_DIM = 64
NA_KR_MAX = 8
NA_KC = 16
A_QK_W = N_DIFF_HEADS * 2 * DIFF_HEAD_DIM
A_V_W = N_DIFF_HEADS * DIFF_V_DIM
B_W = N_NA_HEADS * NA_HEAD_DIM
IN_W = 2 * A_QK_W + A_V_W + 3 * B_W + 2 * D_MODEL
PEER_HEADS = 8
PEER_N_KEYS = 128
PEER_N_EXPERTS = PEER_N_KEYS * PEER_N_KEYS
PEER_QUERY_DIM = 256
PEER_TOPK = 16
PEER_TOKEN_BLOCK = 128
EPS = 1e-6

kernel_name = "hybrid_diffattn_natten_peer_block"

def rmsnorm(x, g):
    xf = x.astype(jnp.float32)
    y = xf * lax.rsqrt(jnp.mean(xf * xf, axis=-1, keepdims=True) + EPS)
    return (y * g.astype(jnp.float32)).astype(x.dtype)

def rope_tables(seq_len):
    inv_freq = ROPE_THETA ** (-jnp.arange(0, ROPE_DIM, 2, dtype=jnp.float32) / ROPE_DIM)
    ang = jnp.arange(seq_len, dtype=jnp.float32)[:, None] * inv_freq[None, :]
    return jnp.cos(ang), jnp.sin(ang)

def apply_partial_rope(x, cos, sin):
    xr, xp = x[..., :ROPE_DIM], x[..., ROPE_DIM:]
    half = ROPE_DIM // 2
    x1, x2 = xr[..., :half], xr[..., half:]
    c, s = cos.astype(x.dtype), sin.astype(x.dtype)
    rot = jnp.concatenate([x1 * c - x2 * s, x2 * c + x1 * s], axis=-1)
    return jnp.concatenate([rot, xp], axis=-1)

def differential_attention(q, k, v, lam, lam_init, subln_g):
    B, S, _ = v.shape
    H, d = N_DIFF_HEADS, DIFF_HEAD_DIM
    q = q.reshape(B, S, H, 2, d).transpose(0, 2, 3, 1, 4)
    k = k.reshape(B, S, H, 2, d).transpose(0, 2, 3, 1, 4)
    v = v.reshape(B, S, H, DIFF_V_DIM).transpose(0, 2, 1, 3)
    cos, sin = rope_tables(S)
    q = apply_partial_rope(q, cos, sin) * (d ** -0.5)
    k = apply_partial_rope(k, cos, sin)
    n_blocks = S // Q_BLOCK
    qb = q.reshape(B, H, 2, n_blocks, Q_BLOCK, d).transpose(3, 0, 1, 2, 4, 5)
    lam_v = lam.astype(v.dtype)

    def block(q_blk):
        s = jnp.einsum('bhmqd,bhmkd->bhmqk', q_blk, k).astype(jnp.float32)
        p = jax.nn.softmax(s, axis=-1).astype(v.dtype)
        a = p[:, :, 0] - lam_v * p[:, :, 1]
        return jnp.einsum('bhqk,bhkv->bhqv', a, v)

    o = lax.map(block, qb)
    o = o.transpose(1, 0, 3, 2, 4).reshape(B, S, H, DIFF_V_DIM)
    o = rmsnorm(o, subln_g) * (1.0 - lam_init)
    return o.reshape(B, S, H * DIFF_V_DIM)

def neighbourhood_attention(q, k, v, rpb):
    B, S, _ = q.shape
    H, d = N_NA_HEADS, NA_HEAD_DIM
    rows = S // GRID_W
    kr = min(NA_KR_MAX, rows)

    def to_grid(t):
        return t.reshape(B, rows, GRID_W, H, d).transpose(0, 3, 1, 2, 4)

    qg = to_grid(q) * (d ** -0.5)
    kg, vg = to_grid(k), to_grid(v)
    cols = jnp.arange(GRID_W)
    col_start = jnp.clip(cols - NA_KC // 2, 0, GRID_W - NA_KC)
    col_idx = col_start[:, None] + jnp.arange(NA_KC)[None, :]
    col_bias_idx = col_idx - cols[:, None] + (NA_KC - 1)

    def row_block(r):
        rs = jnp.clip(r - kr // 2, 0, rows - kr)
        k_rows = lax.dynamic_slice_in_dim(kg, rs, kr, axis=2)
        v_rows = lax.dynamic_slice_in_dim(vg, rs, kr, axis=2)
        k_nb = k_rows[:, :, :, col_idx, :]
        v_nb = v_rows[:, :, :, col_idx, :]
        q_r = lax.dynamic_index_in_dim(qg, r, axis=2, keepdims=False)
        row_bias_idx = rs + jnp.arange(kr) - r + (NA_KR_MAX - 1)
        bias = rpb[:, row_bias_idx[:, None, None], col_bias_idx[None, :, :]]
        bias = bias.transpose(0, 2, 1, 3)
        s = jnp.einsum('bhcd,bhicjd->bhcij', q_r, k_nb) + bias[None]
        s = s.astype(jnp.float32).reshape(B, H, GRID_W, kr * NA_KC)
        p = jax.nn.softmax(s, axis=-1).astype(v.dtype).reshape(B, H, GRID_W, kr, NA_KC)
        return jnp.einsum('bhcij,bhicjd->bhcd', p, v_nb)

    o = lax.map(row_block, jnp.arange(rows))
    return o.transpose(1, 0, 3, 2, 4).reshape(B, S, H * d)

def peer_ffn(x, w_query, sub_keys, expert_u, expert_v):
    B, S, D = x.shape
    TB, PH, K = PEER_TOKEN_BLOCK, PEER_HEADS, PEER_TOPK
    xt = x.reshape(B * S // TB, TB, D)

    def block(xb):
        q = (xb @ w_query).reshape(TB, PH, 2, PEER_QUERY_DIM // 2)
        s = jnp.einsum('thpd,hpkd->thpk', q, sub_keys).astype(jnp.float32)
        v_half, i_half = lax.top_k(s, K)
        cand = v_half[:, :, 0, :, None] + v_half[:, :, 1, None, :]
        cidx = i_half[:, :, 0, :, None] * PEER_N_KEYS + i_half[:, :, 1, None, :]
        top_s, pos = lax.top_k(cand.reshape(TB, PH, K * K), K)
        idx = jnp.take_along_axis(cidx.reshape(TB, PH, K * K), pos, axis=-1)
        g = jax.nn.softmax(top_s, axis=-1).astype(xb.dtype)
        u = expert_u[idx]
        a = jax.nn.gelu(jnp.einsum('td,thkd->thk', xb, u), approximate=False)
        return jnp.einsum('thk,thkd->td', g * a, expert_v[idx])

    return lax.map(block, xt).reshape(B, S, D)

def setup_inputs(seed: int = 0) -> dict:
    key = jax.random.key(seed)
    ks = jax.random.split(key, 20)
    f32 = jnp.float32
    nrm = lambda k, shape, scale: jax.random.normal(k, shape, f32) * scale
    return {
        "x": nrm(ks[0], (BATCH, SEQ, D_MODEL), 1.0),
        "w_in": nrm(ks[1], (DEPTH, D_MODEL, IN_W), D_MODEL ** -0.5),
        "w_proj_a": nrm(ks[2], (DEPTH, A_V_W, D_MODEL), A_V_W ** -0.5),
        "w_proj_b": nrm(ks[3], (DEPTH, B_W, D_MODEL), B_W ** -0.5),
        "w_out": nrm(ks[4], (DEPTH, D_MODEL, D_MODEL), D_MODEL ** -0.5),
        "norm_mix": 1.0 + nrm(ks[5], (DEPTH, D_MODEL), 0.02),
        "norm_ffn": 1.0 + nrm(ks[6], (DEPTH, D_MODEL), 0.02),
        "norm_final": 1.0 + nrm(ks[7], (D_MODEL,), 0.02),
        "lambda_q1": nrm(ks[8], (DEPTH, DIFF_HEAD_DIM), 0.1),
        "lambda_k1": nrm(ks[9], (DEPTH, DIFF_HEAD_DIM), 0.1),
        "lambda_q2": nrm(ks[10], (DEPTH, DIFF_HEAD_DIM), 0.1),
        "lambda_k2": nrm(ks[11], (DEPTH, DIFF_HEAD_DIM), 0.1),
        "diff_subln": 1.0 + nrm(ks[12], (DEPTH, DIFF_V_DIM), 0.02),
        "na_rpb": nrm(ks[13], (DEPTH, N_NA_HEADS, 2 * NA_KR_MAX - 1, 2 * NA_KC - 1), 0.1),
        "peer_w_query": nrm(ks[14], (DEPTH, D_MODEL, PEER_HEADS * PEER_QUERY_DIM), D_MODEL ** -0.5),
        "peer_sub_keys": nrm(ks[15], (DEPTH, PEER_HEADS, 2, PEER_N_KEYS, PEER_QUERY_DIM // 2), (PEER_QUERY_DIM // 2) ** -0.5),
        "peer_u": nrm(ks[16], (DEPTH, PEER_N_EXPERTS, D_MODEL), D_MODEL ** -0.5),
        "peer_v": nrm(ks[17], (DEPTH, PEER_N_EXPERTS, D_MODEL), 0.5),
    }

def reference(x, w_in, w_proj_a, w_proj_b, w_out, norm_mix, norm_ffn, norm_final,
              lambda_q1, lambda_k1, lambda_q2, lambda_k2, diff_subln, na_rpb,
              peer_w_query, peer_sub_keys, peer_u, peer_v):
    split_points = list(np.cumsum([A_QK_W, A_QK_W, A_V_W, B_W, B_W, B_W, D_MODEL])[:])
    h = x
    for l in range(DEPTH):
        lam_init = 0.8 - 0.6 * math.exp(-0.3 * l)
        lam = (jnp.exp(jnp.sum(lambda_q1[l].astype(jnp.float32) * lambda_k1[l].astype(jnp.float32)))
               - jnp.exp(jnp.sum(lambda_q2[l].astype(jnp.float32) * lambda_k2[l].astype(jnp.float32)))
               + lam_init)
        n = rmsnorm(h, norm_mix[l])
        proj = n @ w_in[l]
        qa, ka, va, qb, kb, vb, ga, gb = jnp.split(proj, split_points, axis=-1)
        y_a = differential_attention(qa, ka, va, lam, lam_init, diff_subln[l])
        y_b = neighbourhood_attention(qb, kb, vb, na_rpb[l])
        merged = (jax.nn.sigmoid(ga) * (y_a @ w_proj_a[l])
                  + jax.nn.sigmoid(gb) * (y_b @ w_proj_b[l]))
        h = h + merged @ w_out[l]
        h = h + peer_ffn(rmsnorm(h, norm_ffn[l]), peer_w_query[l], peer_sub_keys[l],
                         peer_u[l], peer_v[l])
    return rmsnorm(h, norm_final)


_drawn_inputs = setup_inputs


def setup_inputs(seed=0):
    import zlib

    import numpy as np

    out = dict(_drawn_inputs(seed))
    spreads = {}
    factors = {'norm_final': 2.866, 'lambda_k1': 4.413, 'lambda_q2': 4.713}
    for name, (base, spread) in spreads.items():
        noise = np.random.default_rng([zlib.crc32(name.encode()), seed]).standard_normal(out[name].shape)
        drawn = base * np.exp(spread * noise) if base else spread * noise
        out[name] = __import__('jax').numpy.asarray(drawn.astype(out[name].dtype))
    for name, factor in factors.items():
        out[name] = (out[name] * factor).astype(out[name].dtype)
    return out
```

```python
from contextlib import ExitStack

import numpy as np

import concourse.bass as bass
from concourse import mybir

F32 = mybir.dt.float32
F32R = mybir.dt.float32r
BF16 = mybir.dt.bfloat16
U32 = mybir.dt.uint32
ALU = mybir.AluOpType
ACT = mybir.ActivationFunctionType
AX_X = mybir.AxisListType.X

P = 128
T = 256
TB = T // P
D = 1024
C = D // P
DH = 64
HA = 4
HB = 8
GRID_W, KC, KR_MAX = 64, 16, 8
ROWS = T // GRID_W
PH, NK, TOPK = 8, 128, 16
HP = PH * 2
EPS = 1e-6
LAM_INIT = 0.8 - 0.6 * float(np.exp(-0.0))
SCALE = DH ** -0.5
SINK = -3.0e38
MASKED = -1.0e30

T_QA, T_KA, T_VA = 0, HA, 2 * HA
T_QB = 3 * HA
T_KB, T_VB = T_QB + 4, T_QB + 8
T_GATE = T_QB + 12
T_PROJ = T_GATE + 16
T_OUT = T_PROJ + C
T_QUERY = T_OUT + C
T_U = T_QUERY + HP
NE_TILES = NK
T_V = T_U + NE_TILES
T_END = T_V + NE_TILES
RAW = 4
RING = 4
LEAD = 3

UNITS_A, UNITS_B = 8, 8
SLOT_A, SLOT_B = T_QB, T_GATE
U_PLAIN = NE_TILES // 2
GTOK = T // (NE_TILES - U_PLAIN)

CONST = {}
_at = 0
for _name, _n in (("ident", P), ("iota", P), ("rot", P), ("ones", P), ("cos", T), ("sin", T), ("iota16", 16), ("mask", GRID_W)):
    CONST[_name] = (_at, _at + _n)
    _at += _n
N_CONST = _at


def unit_slot(n):
    return SLOT_A + n if n < UNITS_A else SLOT_B + n - UNITS_A


def units_at(slot, lag):
    return [n for n in range(UNITS_A + UNITS_B) if unit_slot(n) + lag == slot]


def evac_engine(t):
    dve = lambda x: x < T_VA or T_PROJ <= x < T_QUERY
    same = [x for x in range(t + 1) if dve(x) == dve(t)]
    return dve(t), len(same)


def build(nc, stream, vrows, const, cols, keys, bias, lamv, gfin, h1_dram, a_dram, out):
    with ExitStack() as top:
        def psum(name, shape):
            return top.enter_context(nc.psum_tensor(name, shape, F32))

        def sem(name):
            return top.enter_context(nc.semaphore(name))

        def sbs(stack, name, shape, dt=F32):
            return stack.enter_context(nc.sbuf_tensor(name, shape, dt))

        raw = [sbs(top, f"raw{s}", [P, C, P]) for s in range(RAW)]
        whi = [sbs(top, f"whi{s}", [P, C, P], F32R) for s in range(RING)]
        wlo = [sbs(top, f"wlo{s}", [P, C, P], F32R) for s in range(RING)]
        with ExitStack() as front:
            cst = sbs(front, "cst", [P, N_CONST])
            col = sbs(front, "col", [P, 2 * C + 1])
            xT = sbs(front, "xT", [P, C, T])
            rstd = sbs(front, "rstd", [P, T])
            with ExitStack() as mixer:
                qkT = sbs(mixer, "qkT", [P, 16, T])
                gates = sbs(mixer, "gates", [P, 16, T])
                vtok = sbs(mixer, "vtok", [P, TB, 8, P])
                biasm = sbs(mixer, "biasm", [P, TB, HB, T])
                prob = sbs(mixer, "prob", [P, 2, 2, T])
                dif = sbs(mixer, "dif", [P, 2, T])
                probT = sbs(mixer, "probT", [P, 2, 2 * T])
                rtmp = sbs(mixer, "rtmp", [P, 2, T])
                oA = sbs(mixer, "oA", [P, TB, HA, P])
                oB = sbs(mixer, "oB", [P, TB, HA, P])
                yf = sbs(mixer, "yf", [P, HA, P])
                yhi = sbs(mixer, "yhi", [P, C, T], F32R)
                ylo = sbs(mixer, "ylo", [P, C, T], F32R)
                mtmp = sbs(mixer, "mtmp", [P, 2, T])
                mfull = sbs(mixer, "mfull", [P, 2, T])
                mhi = sbs(mixer, "mhi", [P, C, T], F32R)
                mlo = sbs(mixer, "mlo", [P, C, T], F32R)
            with ExitStack() as router:
                qp = sbs(router, "qp", [P, HP, T])
                qpad = sbs(router, "qpad", [P, 16, T])
                keysT = sbs(router, "keysT", [P, HP, NK])
                sc = sbs(router, "sc", [P, TB, HP, NK])
                scm = sbs(router, "scm", [P, NK])
                top_v = sbs(router, "top_v", [P, TB, HP, TOPK])
                top_i = sbs(router, "top_i", [P, TB, HP, TOPK], U32)
                top_f = sbs(router, "top_f", [P, TB, HP, TOPK])
                cand = sbs(router, "cand", [P, PH, TOPK * TOPK])
                candm = sbs(router, "candm", [P, TOPK * TOPK])
                pick_v = sbs(router, "pick_v", [P, PH, TOPK])
                pick_p = sbs(router, "pick_p", [P, PH, TOPK], U32)
                pick_h = sbs(router, "pick_h", [P, 2, PH, TOPK], U32)
                pick_f = sbs(router, "pick_f", [P, 2, PH, TOPK])
                eq = sbs(router, "eq", [P, PH * TOPK, TOPK])
                route = sbs(router, "route", [P, TB, 3, PH, TOPK])
                gsum = sbs(router, "gsum", [P, 2, PH])
                h1tok = sbs(router, "h1tok", [P, TB, D])
            small = sbs(front, "small", [P, 1])
        G = sbs(top, "G", [P, NK, T])
        mx = sbs(top, "mx", [P, 16, 2])
        nmx = sbs(top, "nmx", [P, 16, 2])
        zs = sbs(top, "zs", [P, 16, 2])
        rz = sbs(top, "rz", [P, 16, 2])
        lam = sbs(top, "lam", [P, 8])
        ssA = sbs(top, "ssA", [P, 2, TB * HA])
        ident = sbs(top, "ident", [P, P])
        iota = sbs(top, "iota", [P, P])
        with ExitStack() as uphase:
            xhi = sbs(uphase, "xhi", [P, C, T], F32R)
            xlo = sbs(uphase, "xlo", [P, C, T], F32R)
            routeT = sbs(uphase, "routeT", [P, 3, T])
            onehot = [sbs(uphase, f"onehot{s}", [P, 2, GTOK, P]) for s in range(2)]
            ast = [sbs(uphase, f"ast{s}", [P, T]) for s in range(2)]
        with ExitStack() as vphase:
            aring = [sbs(vphase, f"aring{s}", [P, T]) for s in range(4)]
            wfull = [sbs(vphase, f"wfull{s}", [P, T]) for s in range(2)]
            ghi = [sbs(vphase, f"ghi{s}", [P, T], F32R) for s in range(2)]
            glo = [sbs(vphase, f"glo{s}", [P, T], F32R) for s in range(2)]
            zero = sbs(vphase, "zero", [P, 512], BF16)
            gf = sbs(vphase, "gf", [P, D])
            htok = sbs(vphase, "htok", [P, TB, D])
            fin = sbs(vphase, "fin", [P, 8])

        def K(name):
            a, b = CONST[name]
            return cst[:, a:b]

        pO = [psum("pO0", [P, 512]), psum("pO1", [P, 512])]
        pSS = psum("pSS", [P, 2, 512])
        pS = [pSS[:, 0, :], pSS[:, 1, :]]
        pT = [psum("pT0", [P, 512]), psum("pT1", [P, 512])]
        pM = [psum("pM0", [P, 512]), psum("pM1", [P, 512])]
        acc = [[pT[0], pT[1]], [pM[0], pM[1]]]

        raw_landed = [sem(f"raw_landed{s}") for s in range(RAW)]
        const_landed = sem("const_landed")
        bias_landed = sem("bias_landed")
        keys_landed = sem("keys_landed")
        hi_ready = sem("hi_ready")
        lo_ready = sem("lo_ready")
        tile_done = sem("tile_done")
        evac_act = sem("evac_act")
        evac_dve = sem("evac_dve")
        dve_order = sem("dve_order")
        act_order = sem("act_order")
        squares = sem("squares")
        ssq_done = sem("ssq_done")
        meansq = sem("meansq")
        root = sem("root")
        normed = sem("normed")
        norm_hi = sem("norm_hi")
        norm_lo = sem("norm_lo")
        lam_sums = sem("lam_sums")
        lam_exps = sem("lam_exps")
        rot_in = sem("rot_in")
        rot_done = sem("rot_done")
        roped = sem("roped")
        bias_masked = sem("bias_masked")
        scores_done = sem("scores_done")
        scores_taken = sem("scores_taken")
        max_ready = sem("max_ready")
        exp_done = sem("exp_done")
        dif_ready = sem("dif_ready")
        probs_turned = sem("probs_turned")
        turned_taken = sem("turned_taken")
        pv_done = sem("pv_done")
        pv_taken = sem("pv_taken")
        ya_meansq = sem("ya_meansq")
        ya_root = sem("ya_root")
        y_ready = sem("y_ready")
        y_turned = sem("y_turned")
        y_full = sem("y_full")
        y_hi = sem("y_hi")
        y_lo = sem("y_lo")
        m_full = sem("m_full")
        m_hi = sem("m_hi")
        m_lo = sem("m_lo")
        h1_turned = sem("h1_turned")
        h1_taken = sem("h1_taken")
        h1_stored = sem("h1_stored")
        key_scores = sem("key_scores")
        sbank_taken = sem("sbank_taken")
        pick_max = sem("pick_max")
        pick_exp = sem("pick_exp")
        routed = sem("routed")
        route_turned = sem("route_turned")
        route_taken = sem("route_taken")
        onehot_ready = sem("onehot_ready")
        g_done = sem("g_done")
        gelu_done = sem("gelu_done")
        a_stored = [sem(f"a_stored{s}") for s in range(2)]
        a_landed = [sem(f"a_landed{s}") for s in range(4)]
        final_landed = sem("final_landed")
        w_ready = sem("w_ready")
        ghi_ready = sem("ghi_ready")
        glo_ready = sem("glo_ready")
        zeroed = sem("zeroed")
        acc_done = sem("acc_done")
        fin_ms = sem("fin_ms")
        fin_root = sem("fin_root")
        out_ready = sem("out_ready")
        out_stored = sem("out_stored")

        block = top.enter_context(nc.Block())
        ngroups = (T_V - RAW) // RAW

        @block.sync
        def _(sp):
            sp.dma_start(xT[:], const["xT"]).then_inc(const_landed, 16)
            sp.dma_start(cst[:], const["cst"]).then_inc(const_landed, 16)
            sp.dma_start(ident[:], const["cst"][:, 0:P]).then_inc(const_landed, 16)
            sp.dma_start(iota[:], const["cst"][:, P:2 * P]).then_inc(const_landed, 16)
            sp.dma_start(col[:], cols).then_inc(const_landed, 16)
            for s in range(4):
                sp.dma_start(rtmp[:, s // 2, (s % 2) * DH:(s % 2 + 1) * DH], lamv[s:s + 1, :].to_broadcast([P, DH])).then_inc(const_landed, 16)
            for t in range(RAW):
                sp.dma_start(raw[t][:], stream[t]).then_inc(raw_landed[t], 16)
            sp.dma_start(biasm[:], bias).then_inc(bias_landed, 16)

            def load(t, s, row):
                sp.wait_ge(lo_ready, t - RAW + 1)
                sp.dma_start(raw[s][:], row).then_inc(raw_landed[s], 16)

            with sp.Fori(1, T_QUERY // RAW + 1) as g:
                for s in range(RAW):
                    load(g * RAW + s, s, stream[bass.ds(g * RAW + s, 1)])
            sp.wait_ge(norm_lo, 2)
            sp.dma_start(keysT[:], keys).then_inc(keys_landed, 16)
            with sp.Fori(T_QUERY // RAW + 1, T_U // RAW) as g:
                for s in range(RAW):
                    load(g * RAW + s, s, stream[bass.ds(g * RAW + s, 1)])
            sp.wait_ge(h1_taken, 4)
            sp.dma_start(h1_dram, h1tok[:]).then_inc(h1_stored, 16)
            with sp.Fori(T_U // RAW, T_V // RAW) as g:
                for s in range(RAW):
                    load(g * RAW + s, s, stream[bass.ds(g * RAW + s, 1)])
            for s in range(RAW):
                load(T_V + s, s, vrows[s:s + 1])
            sp.wait_ge(tile_done, T_V)
            sp.wait_ge(g_done, NE_TILES - U_PLAIN)
            sp.wait_ge(h1_stored, 16)
            for s in range(2):
                sp.wait_ge(a_stored[s], 16 * (NE_TILES // 2))
            for s in range(4):
                sp.dma_start(aring[s][:], a_dram[s]).then_inc(a_landed[s], 16)
            sp.dma_start(gf[:], gfin.to_broadcast([P, D])).then_inc(final_landed, 16)
            sp.dma_start(htok[:], h1_dram).then_inc(final_landed, 16)
            with sp.Fori(1, NE_TILES // RAW) as g:
                for s in range(RAW):
                    load(g * RAW + s + T_V, s, vrows[bass.ds(g * RAW + s, 1)])
                    sp.wait_ge(w_ready, g * RAW + s - 3)
                    sp.dma_start(aring[s][:], a_dram[bass.ds(g * RAW + s, 1)]).then_inc(a_landed[s], 16)
            sp.wait_ge(out_ready, TB)
            sp.dma_start(out, htok[:]).then_inc(out_stored, 16)
            sp.wait_ge(out_stored, 16)

        @block.gpsimd
        def _(pool):
            pool.wait_ge(bias_landed, 16)
            pool.wait_ge(const_landed, 16 * 9)
            bview = biasm[:].rearrange("p b h (r c) -> p (b h r) c", c=GRID_W)
            pool.tensor_tensor(bview, bview, K("mask").unsqueeze(1).to_broadcast([P, TB * HB * ROWS, GRID_W]), ALU.add).then_inc(bias_masked, 1)
            with pool.Fori(0, T_END // RING) as g:
                for s in range(RING):
                    pool.wait_ge(hi_ready, g * RING + s + 1)
                    pool.tensor_tensor(wlo[s][:], raw[s][:], whi[s][:].bitcast(F32), ALU.subtract).then_inc(lo_ready, 1)

        @block.scalar
        def _(act):
            def hi(t, s, turn):
                act.wait_ge(raw_landed[s], turn * 16)
                if isinstance(t, int) and t < RING:
                    pass
                else:
                    act.wait_ge(tile_done, t - RING + 1)
                act.activation(whi[s][:], raw[s][:], ACT.Copy).then_inc(hi_ready, 1)

            def hi_at(t):
                if t < T_END:
                    hi(t, t % RING, t // RAW + 1)

            def norm(k, full, sq):
                act.wait_ge(meansq, k)
                act.activation(rstd[:], rstd[:], ACT.Sqrt).then_inc(root, 1)
                for c in range(C):
                    act.wait_ge(normed, C * (k - 1) + c + 1)
                    act.activation(xhi[:, c, :], full[:, c, :], ACT.Copy).then_inc(norm_hi, 1)

            act.wait_ge(const_landed, 16 * 9)
            act.activation(gates[:, 0:C, :], xT[:], ACT.Square).then_inc(squares, 1)
            for t in range(LEAD):
                hi_at(t)
            act.wait_ge(lam_sums, 1)
            act.activation(lam[:, 2:4], lam[:, 0:2], ACT.Exp).then_inc(lam_exps, 1)
            norm(1, qkT, gates)
            for k in range(T_PROJ):
                hi_at(k + LEAD)
                if k >= T_VA:
                    act.wait_ge(tile_done, k + 1)
                    src = pO[k % 2][:, 0:T]
                    if k >= T_GATE:
                        act.activation(gates[:, k - T_GATE, :], src, ACT.Tanh, scale=0.5).then_inc(evac_act, 1)
                    elif T_VA <= k < T_QB or T_VB <= k:
                        v = k - T_VA if k < T_QB else k - T_VB + HA
                        act.activation(vtok[:, :, v, :], src.rearrange("p (b n) -> p b n", b=TB), ACT.Copy).then_inc(evac_act, 1)
                    else:
                        act.activation(qkT[:, k - T_QB + 8, :], src, ACT.Copy).then_inc(evac_act, 1)
                for n in units_at(k, 0):
                    act.wait_ge(max_ready, n + 1)
                    if n >= 2:
                        if n - 2 < UNITS_A:
                            act.wait_ge(dif_ready, n - 1)
                        else:
                            act.wait_ge(probs_turned, n - 1)
                    for m in range(2):
                        src, scale = (pS[m][:, 0:T], SCALE) if n < UNITS_A else (prob[:, n % 2, m, :], 1.0)
                        act.activation(prob[:, n % 2, m, :], src, ACT.Exp, bias=nmx[:, n, m:m + 1], scale=scale,
                                       accum_out=zs[:, n, m:m + 1]).then_inc(exp_done, 1)
                if k == T_GATE - 1:
                    act.wait_ge(ya_meansq, 1)
                    act.activation(ssA[:, 0, :], ssA[:, 0, :], ACT.Sqrt).then_inc(ya_root, 1)
                if k in (T_GATE, T_GATE + 1, T_PROJ - 3, T_PROJ - 2):
                    j = {T_GATE: 0, T_GATE + 1: 1, T_PROJ - 3: 2, T_PROJ - 2: 3}[k]
                    act.wait_ge(y_full, j + 1)
                    half, b = j // 2, j % 2
                    act.activation(yhi[:, half * HA:(half + 1) * HA, b * P:(b + 1) * P], yf[:], ACT.Copy).then_inc(y_hi, 1)
            for k in range(T_PROJ, T_QUERY):
                hi_at(k + LEAD)
                if k < T_OUT:
                    j = k - T_PROJ
                    act.wait_ge(m_full, j + 1)
                    act.activation(mhi[:, j, :], mfull[:, j % 2, :], ACT.Copy).then_inc(m_hi, 1)
            for c in range(C):
                act.wait_ge(evac_dve, evac_engine(T_OUT + c)[1])
                act.activation(gates[:, c, :], xT[:, c, :], ACT.Square).then_inc(squares, 1)
            norm(2, qkT, gates)
            for k in range(T_QUERY, T_U):
                hi_at(k + LEAD)
                act.wait_ge(tile_done, k + 1)
                act.activation(qp[:, k - T_QUERY, :], pO[k % 2][:, 0:T], ACT.Copy).then_inc(evac_act, 1)
                if k >= T_QUERY + 4 and (k - T_QUERY) % 2 == 1:
                    pass
            act.preload_act_table(ACT.Gelu)

            def gelu(t, i, s2, turns):
                act.wait_ge(tile_done, t + 1)
                if turns is not None:
                    act.wait_ge(a_stored[s2], turns)
                act.activation(ast[s2][:], pO[s2][:, 0:T], ACT.Gelu).then_inc(evac_act, 1)

            def store(i, s2, count):
                act.wait_ge(evac_act, count)
                act.dma_start(a_dram[bass.ds(i, 1)] if not isinstance(i, int) else a_dram[i], ast[s2][:]).then_inc(a_stored[s2], 16)

            base = evac_engine(T_U - 1)[1]

            for i in range(8):
                hi_at(T_U + i + LEAD)
                n = i
                act.wait_ge(key_scores, n + 1)
                b, q4 = n // 4, n % 4
                act.activation(sc[:, b, q4 * 4:(q4 + 1) * 4, :], pS[n % 2].rearrange("p (h k) -> p h k", h=4), ACT.Copy).then_inc(sbank_taken, 1)
                gelu(T_U + i, i, i % 2, None if i < 2 else 16 * (i // 2))
                store(i, i % 2, base + i + 1)
            place_exp = {20: 0, 40: 1}
            i0 = 8
            for stop in (20, 40, U_PLAIN):
                with act.Fori(i0 // 4, stop // 4) as g:
                    for s in range(4):
                        i = g * 4 + s
                        hi(i + (T_U + LEAD), (s + LEAD) % RING, g + (T_U // RAW + (s + LEAD) // RAW + 1))
                        gelu(i + T_U, i, s % 2, (g * 2 + s // 2) * 16)
                        store(i, s % 2, i + (base + 1))
                if stop in place_exp:
                    b = place_exp[stop]
                    act.wait_ge(pick_max, b + 1)
                    act.activation(route[:, b, 2, :, :], route[:, b, 2, :, :], ACT.Exp).then_inc(pick_exp, 1)
                    act.preload_act_table(ACT.Gelu)
                i0 = stop
            with act.Fori(U_PLAIN // 4, NE_TILES // 4) as g:
                for s in range(4):
                    i = g * 4 + s
                    hi(i + (T_U + LEAD), (s + LEAD) % RING, g + (T_U // RAW + (s + LEAD) // RAW + 1))
                    gelu(i + T_U, i, s % 2, (g * 2 + s // 2) * 16)
                    store(i, s % 2, i + (base + 1))
                    act.wait_ge(g_done, i - U_PLAIN + 1)
                    act.activation(G[:, :, bass.ds((i - U_PLAIN) * GTOK, GTOK)].rearrange("p i t -> p t i"),
                                   pS[s % 2].rearrange("p (t i) -> p t i", t=GTOK), ACT.Copy).then_inc(sbank_taken, 1)

            def w_hi(i, s):
                act.wait_ge(w_ready, i + 1)
                act.wait_ge(tile_done, i + (T_V - 1))
                act.activation(ghi[s % 2][:], wfull[s % 2][:], ACT.Copy).then_inc(ghi_ready, 1)

            with act.Fori(0, NE_TILES // 4 - 1) as g:
                for s in range(4):
                    w_hi(g * 4 + s, s)
                    hi(g * 4 + (s + T_V + LEAD), (s + LEAD) % RING, g + (T_V // RAW + (s + LEAD) // RAW + 1))
            for i in range(NE_TILES - 4, NE_TILES):
                w_hi(i, i)
                hi_at(T_V + i + LEAD)
            act.wait_ge(fin_ms, 1)
            act.activation(fin[:, 2:4], fin[:, 0:2], ACT.Sqrt).then_inc(fin_root, 1)

        @block.vector
        def _(dve):
            order = [0]

            def link(ins):
                order[0] += 1
                ins.then_inc(dve_order, 1)
                dve.wait_ge(dve_order, order[0])

            def norm(k, gain0, full):
                dve.wait_ge(ssq_done, k)
                dve.tensor_scalar(rstd[:], pM[0][:, 0:T], 1.0 / D, EPS, ALU.mult, ALU.add).then_inc(meansq, 1)
                dve.wait_ge(root, k)
                link(dve.reciprocal(rstd[:], rstd[:]))
                for c in range(C):
                    dve.scalar_tensor_tensor(full[:, c, :], xT[:, c, :], col[:, gain0 + c:gain0 + c + 1], rstd[:],
                                             ALU.mult, ALU.mult).then_inc(normed, 1)
                dve.wait_ge(normed, C * k)
                for c in range(C):
                    dve.wait_ge(norm_hi, C * (k - 1) + c + 1)
                    ins = dve.tensor_tensor(xlo[:, c, :], full[:, c, :], xhi[:, c, :].bitcast(F32), ALU.subtract)
                    if c == C - 1:
                        ins.then_inc(norm_lo, 1)

            dve.wait_ge(const_landed, 16 * 9)
            for m in range(2):
                link(dve.tensor_tensor(mtmp[:, m, 0:DH], rtmp[:, m, 0:DH], rtmp[:, m, DH:2 * DH], ALU.mult))
            dve.tensor_reduce(lam[:, 0:2], mtmp[:, :, 0:DH], AX_X, ALU.add).then_inc(lam_sums, 1)
            dve.wait_ge(lam_exps, 1)
            link(dve.tensor_tensor(lam[:, 4:5], lam[:, 3:4], lam[:, 2:3], ALU.subtract))
            link(dve.tensor_scalar(lam[:, 5:6], lam[:, 4:5], -LAM_INIT, None, ALU.add))
            link(dve.tensor_scalar(lam[:, 6:7], col[:, 2 * C:2 * C + 1], 1.0 - LAM_INIT, None, ALU.mult))
            norm(1, 0, qkT)
            dve.wait_ge(norm_lo, 1)

            def take_turned(n):
                if n >= 2:
                    dve.wait_ge(pv_done, n - 1)
                dve.wait_ge(probs_turned, n + 1)
                w = T if n < UNITS_A else 2 * T
                dve.tensor_copy(probT[:, n % 2, 0:w], pT[n % 2][:, 0:w]).then_inc(turned_taken, 1)

            def take_pv(n):
                dve.wait_ge(pv_done, n + 1)
                if n < UNITS_A:
                    h, b = n % HA, n // HA
                    dve.tensor_copy(oA[:, b, h, :], pM[n % 2][:, 0:P]).then_inc(pv_taken, 1)
                else:
                    h, b = (n - UNITS_A) % HA, (n - UNITS_A) // HA
                    dve.tensor_tensor(oB[:, b, h, :].rearrange("p (m v) -> p m v", m=2),
                                      pM[n % 2][:, 0:P].rearrange("p (m v) -> p m v", m=2),
                                      rz[:, n, :].unsqueeze(2).to_broadcast([P, 2, DH]), ALU.mult).then_inc(pv_taken, 1)

            def y_parts(j):
                half, b = j // 2, j % 2
                dve.wait_ge(y_turned, j + 1)
                if j:
                    dve.wait_ge(y_lo, j)
                src = pT[j % 2][:].rearrange("p (h t) -> p h t", h=HA)
                if half == 0:
                    dve.tensor_scalar(yf[:], src, lam[:, 6:7], None, ALU.mult).then_inc(y_full, 1)
                else:
                    dve.tensor_copy(yf[:], src).then_inc(y_full, 1)
                dve.wait_ge(y_full, j + 1)
                dve.wait_ge(y_hi, j + 1)
                at = (slice(None), slice(half * HA, (half + 1) * HA), slice(b * P, (b + 1) * P))
                dve.tensor_tensor(ylo[at], yf[:], yhi[at].bitcast(F32), ALU.subtract).then_inc(y_lo, 1)

            for k in range(T_PROJ + 1):
                if k < T_VA:
                    dve.wait_ge(tile_done, k + 1)
                    dve.tensor_copy(qkT[:, k, :], pO[k % 2][:, 0:T]).then_inc(evac_dve, 1)
                    dve.wait_ge(evac_dve, k + 1)
                    link(dve.tensor_tensor(rtmp[:, 0, :], qkT[:, k, :], K("cos"), ALU.mult))
                    dve.wait_ge(rot_done, k + 1)
                    link(dve.tensor_tensor(rtmp[:, 1, :], pM[k % 2][:, 0:T], K("sin"), ALU.mult))
                    dve.tensor_tensor(qkT[:, k, :], rtmp[:, 0, :], rtmp[:, 1, :], ALU.add).then_inc(roped, 1)
                    dve.wait_ge(roped, k + 1)
                for n in units_at(k, 1):
                    dve.wait_ge(exp_done, 2 * (n + 1))
                    if n < UNITS_A:
                        link(dve.reciprocal(rz[:, n, :], zs[:, n, :]))
                        link(dve.tensor_tensor(rz[:, n, 1:2], rz[:, n, 1:2], lam[:, 5:6], ALU.mult))
                        if n >= 2:
                            dve.wait_ge(probs_turned, n - 1)
                        link(dve.tensor_scalar(rtmp[:, 0, :], prob[:, n % 2, 1, :], rz[:, n, 1:2], None, ALU.mult))
                        dve.scalar_tensor_tensor(dif[:, n % 2, :], prob[:, n % 2, 0, :], rz[:, n, 0:1], rtmp[:, 0, :],
                                                 ALU.mult, ALU.add).then_inc(dif_ready, 1)
                        dve.wait_ge(dif_ready, n + 1)
                    else:
                        link(dve.reciprocal(rz[:, n, :], zs[:, n, :]))
                for n in units_at(k, 0):
                    dve.wait_ge(scores_done, n + 1)
                    if n < UNITS_A:
                        link(dve.tensor_reduce(mx[:, n, :], pSS[:, :, 0:T], AX_X, ALU.max))
                        dve.tensor_scalar(nmx[:, n, :], mx[:, n, :], -SCALE, None, ALU.mult).then_inc(max_ready, 1)
                    else:
                        h, b = (n - UNITS_A) % HA, (n - UNITS_A) // HA
                        if n == UNITS_A:
                            dve.wait_ge(bias_masked, 1)
                        if n - 2 >= UNITS_A:
                            dve.wait_ge(probs_turned, n - 1)
                        dve.scalar_tensor_tensor(prob[:, n % 2, :, :], pSS[:, :, 0:T], SCALE,
                                                 biasm[:, b, 2 * h:2 * h + 2, :], ALU.mult, ALU.add).then_inc(scores_taken, 1)
                        dve.wait_ge(scores_taken, n - UNITS_A + 1)
                        link(dve.tensor_reduce(mx[:, n, :], prob[:, n % 2, :, :], AX_X, ALU.max))
                        dve.tensor_scalar(nmx[:, n, :], mx[:, n, :], -1.0, None, ALU.mult).then_inc(max_ready, 1)
                for n in units_at(k, 2):
                    take_turned(n)
                for n in units_at(k, 3):
                    take_pv(n)
                if k == T_GATE - 1:
                    dve.wait_ge(pv_taken, UNITS_A)
                    flat = oA[:].rearrange("p b h v -> p (b h) v")
                    sq = mhi_free = gates[:, 0:4, :].rearrange("p a b -> p (a b)").rearrange("p (u v) -> p u v", v=P)
                    link(dve.tensor_tensor(sq, flat, flat, ALU.mult))
                    link(dve.tensor_reduce(ssA[:, 1, :], sq, AX_X, ALU.add))
                    dve.tensor_scalar(ssA[:, 0, :], ssA[:, 1, :], 1.0 / P, EPS, ALU.mult, ALU.add).then_inc(ya_meansq, 1)
                    dve.wait_ge(ya_root, 1)
                    link(dve.reciprocal(ssA[:, 1, :], ssA[:, 0, :]))
                    dve.tensor_tensor(flat, flat, ssA[:, 1, :].unsqueeze(2).to_broadcast([P, TB * HA, P]), ALU.mult).then_inc(y_ready, 1)
                if k in (T_GATE, T_GATE + 1):
                    y_parts(k - T_GATE)
                if k in (T_PROJ - 3, T_PROJ - 2):
                    y_parts(k - T_PROJ + 5)
            for k in range(T_PROJ, T_OUT):
                j = k - T_PROJ
                dve.wait_ge(tile_done, k + 1)
                if j == 0:
                    dve.wait_ge(evac_act, evac_engine(T_PROJ - 1)[1])
                link(dve.scalar_tensor_tensor(mtmp[:, 0, :], gates[:, j, :], 1.0, pO[k % 2][:, 0:T], ALU.add, ALU.mult))
                dve.scalar_tensor_tensor(mtmp[:, 1, :], gates[:, C + j, :], 1.0, pO[k % 2][:, T:2 * T], ALU.add, ALU.mult).then_inc(evac_dve, 1)
                dve.wait_ge(evac_dve, evac_engine(k)[1])
                dve.tensor_tensor(mfull[:, j % 2, :], mtmp[:, 0, :], mtmp[:, 1, :], ALU.add).then_inc(m_full, 1)
                dve.wait_ge(m_full, j + 1)
                dve.wait_ge(m_hi, j + 1)
                dve.tensor_tensor(mlo[:, j, :], mfull[:, j % 2, :], mhi[:, j, :].bitcast(F32), ALU.subtract).then_inc(m_lo, 1)
                dve.wait_ge(m_lo, j + 1)
            for k in range(T_OUT, T_QUERY):
                j = k - T_OUT
                dve.wait_ge(tile_done, k + 1)
                dve.scalar_tensor_tensor(xT[:, j, :], pO[k % 2][:, 0:T], 0.5, xT[:, j, :], ALU.mult, ALU.add).then_inc(evac_dve, 1)
            dve.wait_ge(evac_dve, evac_engine(T_QUERY - 1)[1])
            norm(2, C, qkT)
            dve.wait_ge(norm_lo, 2)
            for j in range(4):
                dve.wait_ge(h1_turned, j + 1)
                b, q = j // 2, j % 2
                dve.tensor_copy(h1tok[:, b, q * 512:(q + 1) * 512], pT[j % 2][:]).then_inc(h1_taken, 1)

            def top16(vals, idx, src, work):
                link(dve.max(vals[:, 0:8], src))
                dve.max_index(idx[:, 0:8], vals[:, 0:8], src)
                link(dve.match_replace(work, vals[:, 0:8], src, SINK))
                link(dve.max(vals[:, 8:16], work))
                link(dve.max_index(idx[:, 8:16], vals[:, 8:16], work))

            for b in range(TB):
                for h in range(HP):
                    if h % 4 == 0:
                        dve.wait_ge(sbank_taken, b * 4 + h // 4 + 1)
                    top16(top_v[:, b, h, :], top_i[:, b, h, :], sc[:, b, h, :], scm[:])
                link(dve.tensor_copy(top_f[:, b], top_i[:, b]))
                halves = top_v[:, b].rearrange("p (h q) k -> p q h k", q=2)
                for h in range(PH):
                    ins = dve.tensor_tensor(cand[:, h, :].rearrange("p (x y) -> p x y", x=TOPK),
                                            top_v[:, b, 2 * h, :].unsqueeze(2).to_broadcast([P, TOPK, TOPK]),
                                            top_v[:, b, 2 * h + 1, :].unsqueeze(1).to_broadcast([P, TOPK, TOPK]), ALU.add)
                    link(ins)
                for h in range(PH):
                    top16(pick_v[:, h, :], pick_p[:, h, :], cand[:, h, :], candm[:])
                dve.tensor_tensor(route[:, b, 2], pick_v[:], pick_v[:, :, 0:1].to_broadcast([P, PH, TOPK]), ALU.subtract).then_inc(pick_max, 1)
                link(dve.tensor_scalar(pick_h[:, 0], pick_p[:], 4, None, ALU.logical_shift_right))
                link(dve.tensor_scalar(pick_h[:, 1], pick_p[:], TOPK - 1, None, ALU.bitwise_and))
                link(dve.tensor_copy(pick_f[:], pick_h[:]))
                for q in range(2):
                    link(dve.tensor_tensor(eq[:], pick_f[:, q].rearrange("p h k -> p (h k)").unsqueeze(2).to_broadcast([P, PH * TOPK, TOPK]),
                                           K("iota16").unsqueeze(1).to_broadcast([P, PH * TOPK, TOPK]), ALU.is_equal))
                    for h in range(PH):
                        e3 = eq[:, h * TOPK:(h + 1) * TOPK, :]
                        ins = dve.tensor_tensor(e3, e3, top_f[:, b, 2 * h + q, :].unsqueeze(1).to_broadcast([P, TOPK, TOPK]), ALU.mult)
                        link(ins)
                    link(dve.tensor_reduce(route[:, b, q].rearrange("p h k -> p (h k)"), eq[:], AX_X, ALU.add))
                dve.wait_ge(pick_exp, b + 1)
                link(dve.tensor_reduce(gsum[:, 0, :], route[:, b, 2], AX_X, ALU.add))
                link(dve.reciprocal(gsum[:, 1, :], gsum[:, 0, :]))
                dve.tensor_tensor(route[:, b, 2], route[:, b, 2], gsum[:, 1, :].unsqueeze(2).to_broadcast([P, PH, TOPK]), ALU.mult).then_inc(routed, 1)
            for b in range(TB):
                dve.wait_ge(route_turned, b + 1)
                dve.tensor_copy(routeT[:, :, b * P:(b + 1) * P], pM[b][:, 0:3 * P].rearrange("p (a t) -> p a t", a=3)).then_inc(route_taken, 1)
            dve.wait_ge(route_taken, 2)

            def one_hots(k, s):
                def row(a):
                    return routeT[:, a, bass.ds(k * GTOK, GTOK)].unsqueeze(2).to_broadcast([P, GTOK, P])
                io = iota[:].unsqueeze(1).to_broadcast([P, GTOK, P])
                dve.tensor_tensor(onehot[s][:, 1], row(1), io, ALU.is_equal).then_inc(dve_order, 1)
                dve.tensor_tensor(onehot[s][:, 0], row(0), io, ALU.is_equal).then_inc(dve_order, 1)
                dve.wait_ge(dve_order, k * 2 + (order[0] + 2))
                dve.tensor_tensor(onehot[s][:, 1], onehot[s][:, 1], row(2), ALU.mult).then_inc(onehot_ready, 1)

            one_hots(0, 0)
            one_hots(1, 1)
            n_steps = NE_TILES - U_PLAIN
            with dve.Fori(1, n_steps // 2) as g:
                for s in range(2):
                    dve.wait_ge(g_done, g * 2 + s - 1)
                    one_hots(g * 2 + s, s)
            order[0] += 2 * n_steps

            dve.wait_ge(g_done, n_steps)
            dve.wait_ge(tile_done, T_V)
            for s in range(2):
                dve.wait_ge(a_stored[s], 16 * (NE_TILES // 2))
            dve.memset(zero[:], 0.0).then_inc(zeroed, 1)
            dve.wait_ge(sbank_taken, 8 + n_steps)

            def weights(i, s, turn):
                dve.wait_ge(a_landed[s], turn * 16)
                dve.tensor_tensor(wfull[s % 2][:], aring[s][:], G[:, i, :] if isinstance(i, int) else G[:, bass.ds(i, 1), :], ALU.mult).then_inc(w_ready, 1)

            def low(i, s):
                dve.wait_ge(w_ready, i + 1)
                dve.wait_ge(ghi_ready, i + 1)
                dve.tensor_tensor(glo[s % 2][:], wfull[s % 2][:], ghi[s % 2][:].bitcast(F32), ALU.subtract).then_inc(glo_ready, 1)

            weights(0, 0, 1)
            weights(1, 1, 1)
            with dve.Fori(0, NE_TILES // 4 - 1) as g:
                for s in range(4):
                    low(g * 4 + s, s)
                    dve.wait_ge(glo_ready, g * 4 + s + 1)
                    weights(g * 4 + s + 2, (s + 2) % 4, g + ((s + 2) // 4 + 1))
            for i in range(NE_TILES - 4, NE_TILES):
                low(i, i)
                dve.wait_ge(glo_ready, i + 1)
                if i + 2 < NE_TILES:
                    weights(i + 2, (i + 2) % 4, (i + 2) // 4 + 1)

            dve.wait_ge(final_landed, 32)
            dve.wait_ge(acc_done, 1)
            for b in range(TB):
                for q in range(2):
                    link(dve.tensor_tensor(htok[:, b, q * 512:(q + 1) * 512], acc[b][q][:], htok[:, b, q * 512:(q + 1) * 512], ALU.add))
            for b in range(TB):
                sq = G[:, 0:4, :].rearrange("p a b -> p (a b)")
                link(dve.tensor_tensor(sq, htok[:, b], htok[:, b], ALU.mult))
                link(dve.tensor_reduce(fin[:, 4 + b:5 + b], sq, AX_X, ALU.add))
            dve.tensor_scalar(fin[:, 0:2], fin[:, 4:6], 1.0 / D, EPS, ALU.mult, ALU.add).then_inc(fin_ms, 1)
            dve.wait_ge(fin_root, 1)
            link(dve.reciprocal(fin[:, 6:8], fin[:, 2:4]))
            for b in range(TB):
                dve.scalar_tensor_tensor(htok[:, b], htok[:, b], fin[:, 6 + b:7 + b], gf[:], ALU.mult, ALU.mult).then_inc(out_ready, 1)

        @block.tensor
        def _(pe):
            def split_product(dst, terms):
                last = None
                for c, (sh, sl, mh, ml) in enumerate(terms):
                    for q, (st, mv) in enumerate(((sh, mh), (sh, ml), (sl, mh))):
                        last = pe.matmul(dst, st, mv, start=(c == 0 and q == 0), stop=(c == len(terms) - 1 and q == 2))
                return last

            def tile_wait(t):
                pe.wait_ge(lo_ready, t + 1)
                if t >= 2:
                    by_dve, count = evac_engine(t - 2)
                    pe.wait_ge(evac_dve if by_dve else evac_act, count)

            def tile(s, bank, mh, ml):
                return split_product(pO[bank][:, 0:T], [(whi[s][:, c, :], wlo[s][:, c, :], mh[:, c, :], ml[:, c, :]) for c in range(C)])

            def token_tile(s, bank):
                last = None
                for b in range(TB):
                    tok = slice(b * P, (b + 1) * P)
                    last = split_product(pO[bank][:, tok], [(xhi[:, c, tok], xlo[:, c, tok], whi[s][:, c, :], wlo[s][:, c, :]) for c in range(C)])
                return last

            def sum_of_squares(k):
                last = None
                for c in range(C):
                    pe.wait_ge(squares, 1 if k == 1 else 1 + c + 1)
                    last = pe.matmul(pM[0][:, 0:T], K("ones"), gates[:, c, :], start=c == 0, stop=c == C - 1)
                last.then_inc(ssq_done, 1)

            def rotate(k):
                pe.wait_ge(evac_dve, k + 1)
                if k >= 2:
                    pe.wait_ge(roped, k - 1)
                pe.matmul(pM[k % 2][:, 0:T], K("rot"), qkT[:, k, :], start=True, stop=True).then_inc(rot_done, 1)

            def scores(n):
                if 1 <= n <= UNITS_A:
                    pe.wait_ge(exp_done, 2 * n)
                elif n > UNITS_A:
                    pe.wait_ge(scores_taken, n - UNITS_A)
                last = None
                u = n if n < UNITS_A else n - UNITS_A
                h, b = u % HA, u // HA
                q0, k0 = (0, HA) if n < UNITS_A else (8, 12)
                if n == 0:
                    pe.wait_ge(roped, 2 * HA)
                if n == UNITS_A:
                    pe.wait_ge(evac_act, evac_engine(T_GATE - 1)[1])
                for m in range(2):
                    rows = slice(m * DH, (m + 1) * DH)
                    last = pe.matmul(pS[m][:, 0:T], qkT[rows, q0 + h, b * P:(b + 1) * P], qkT[rows, k0 + h, :],
                                     start=True, stop=True)
                last.then_inc(scores_done, 1)

            def turn(n):
                if n == 0:
                    pass
                if n >= 2:
                    pe.wait_ge(turned_taken, n - 1)
                last = None
                if n < UNITS_A:
                    pe.wait_ge(dif_ready, n + 1)
                    for kb in range(TB):
                        last = pe.transpose(pT[n % 2][:, kb * P:(kb + 1) * P], dif[:, n % 2, kb * P:(kb + 1) * P], ident[:])
                else:
                    pe.wait_ge(exp_done, 2 * (n + 1))
                    if n < UNITS_A + 2:
                        pe.wait_ge(y_full, 2)
                    for m in range(2):
                        for kb in range(TB):
                            last = pe.transpose(pT[n % 2][:, m * T + kb * P:m * T + (kb + 1) * P], prob[:, n % 2, m, kb * P:(kb + 1) * P], ident[:])
                last.then_inc(probs_turned, 1)

            def times_v(n):
                pe.wait_ge(turned_taken, n + 1)
                if n >= 2:
                    pe.wait_ge(pv_taken, n - 1)
                last = None
                if n == 0:
                    pe.wait_ge(evac_act, evac_engine(T_QB - 1)[1])
                if n < UNITS_A:
                    for kb in range(TB):
                        last = pe.matmul(pM[n % 2][:, 0:P], probT[:, n % 2, kb * P:(kb + 1) * P], vtok[:, kb, n % HA, :],
                                         start=kb == 0, stop=kb == TB - 1)
                else:
                    pair = (n - UNITS_A) % HA
                    for m in range(2):
                        for kb in range(TB):
                            last = pe.matmul(pM[n % 2][:, m * DH:(m + 1) * DH], probT[:, n % 2, m * T + kb * P:m * T + (kb + 1) * P],
                                             vtok[:, kb, HA + pair, m * DH:(m + 1) * DH], start=kb == 0, stop=kb == TB - 1)
                last.then_inc(pv_done, 1)

            def turn_y(j):
                half, b = j // 2, j % 2
                if half == 0:
                    pe.wait_ge(y_ready, 1)
                    pe.wait_ge(turned_taken, UNITS_A)
                else:
                    pe.wait_ge(pv_taken, UNITS_A + UNITS_B)
                    pe.wait_ge(turned_taken, UNITS_A + UNITS_B)
                src = oA if half == 0 else oB
                last = None
                for h in range(HA):
                    last = pe.transpose(pT[j % 2][:, h * P:(h + 1) * P], src[:, b, h, :], ident[:])
                last.then_inc(y_turned, 1)

            pe.wait_ge(const_landed, 16 * 9)
            sum_of_squares(1)
            pe.wait_ge(norm_lo, 1)
            pe.wait_ge(norm_hi, C)
            for k in range(T_PROJ):
                tile_wait(k)
                if T_VA <= k < T_QB or T_VB <= k < T_GATE:
                    last = token_tile(k % RING, k % 2)
                else:
                    last = tile(k % RING, k % 2, xhi, xlo)
                last.then_inc(tile_done, 1)
                if 1 <= k <= T_VA:
                    rotate(k - 1)
                for n in units_at(k, 0):
                    scores(n)
                for n in units_at(k, 2):
                    turn(n)
                for n in units_at(k, 3):
                    times_v(n)
                if k in (T_GATE, T_GATE + 1):
                    turn_y(k - T_GATE)
                if k in (T_PROJ - 3, T_PROJ - 2):
                    turn_y(k - T_PROJ + 5)
            pe.wait_ge(y_lo, 4)
            pe.wait_ge(y_hi, 4)
            for k in range(T_PROJ, T_OUT):
                tile_wait(k)
                s = k % RING
                for half in range(2):
                    last = split_product(pO[k % 2][:, half * T:(half + 1) * T],
                                         [(whi[s][:, c, :], wlo[s][:, c, :], yhi[:, c, :], ylo[:, c, :]) for c in range(half * HA, (half + 1) * HA)])
                last.then_inc(tile_done, 1)
            pe.wait_ge(m_hi, C)
            pe.wait_ge(m_lo, C)
            for k in range(T_OUT, T_QUERY):
                tile_wait(k)
                tile(k % RING, k % 2, mhi, mlo).then_inc(tile_done, 1)
            sum_of_squares(2)
            for j in range(4):
                b, q = j // 2, j % 2
                if j >= 2:
                    pe.wait_ge(h1_taken, j - 1)
                for c in range(4):
                    last = pe.transpose(pT[j % 2][:, c * P:(c + 1) * P], xT[:, q * 4 + c, b * P:(b + 1) * P], ident[:])
                last.then_inc(h1_turned, 1)
            pe.wait_ge(norm_hi, 2 * C)
            pe.wait_ge(norm_lo, 2)
            for k in range(T_QUERY, T_U):
                tile_wait(k)
                tile(k % RING, k % 2, xhi, xlo).then_inc(tile_done, 1)
            pe.wait_ge(keys_landed, 16)
            pe.wait_ge(evac_act, evac_engine(T_U - 1)[1])
            n = 0
            for i in range(8):
                b, q4 = i // 4, i % 4
                if i >= 2:
                    pe.wait_ge(sbank_taken, i - 1)
                for h in range(4):
                    hp = q4 * 4 + h
                    last = pe.matmul(pS[i % 2][:, h * P:(h + 1) * P], qp[:, hp, b * P:(b + 1) * P], keysT[:, hp, :], start=True, stop=True)
                last.then_inc(key_scores, 1)
                tile_wait(T_U + i)
                tile((T_U + i) % RING, i % 2, xhi, xlo).then_inc(tile_done, 1)

            base = evac_engine(T_U - 1)[1]

            def u_tiles(start, stop, with_g):
                with pe.Fori(start // RING, stop // RING) as g:
                    for s in range(RING):
                        i = g * RING + s
                        pe.wait_ge(lo_ready, i + (T_U + 1))
                        pe.wait_ge(evac_act, i + (base - 1))
                        tile(s, s % 2, xhi, xlo).then_inc(tile_done, 1)
                        if with_g:
                            pe.wait_ge(onehot_ready, i - U_PLAIN + 1)
                            pe.wait_ge(sbank_taken, i - U_PLAIN + 7)
                            for tok in range(GTOK):
                                last = pe.matmul(pS[s % 2][:, tok * P:(tok + 1) * P], onehot[s % 2][:, 1, tok, :], onehot[s % 2][:, 0, tok, :],
                                                 start=True, stop=True)
                            last.then_inc(g_done, 1)

            def turn_route(b):
                pe.wait_ge(routed, b + 1)
                for a in range(3):
                    last = pe.transpose(pM[b][:, a * P:(a + 1) * P], route[:, b, a].rearrange("p h k -> p (h k)"), ident[:])
                last.then_inc(route_turned, 1)

            u_tiles(8, U_PLAIN, False)
            turn_route(0)
            turn_route(1)
            u_tiles(U_PLAIN, NE_TILES, True)

            pe.wait_ge(zeroed, 1)
            pe.wait_ge(route_taken, 2)
            pe.wait_ge(h1_taken, 4)
            for b in range(TB):
                for q in range(2):
                    pe.matmul(acc[b][q][:], zero[:, 0:P], zero[:], start=True, stop=False)
            with pe.Fori(0, NE_TILES // RING) as g:
                for s in range(RING):
                    pe.wait_ge(lo_ready, g * RING + (s + T_V + 1))
                    pe.wait_ge(glo_ready, g * RING + s + 1)
                    vh = whi[s][:].rearrange("p c n -> p (c n)")
                    vl = wlo[s][:].rearrange("p c n -> p (c n)")
                    for b in range(TB):
                        wh, wl = ghi[s % 2][:, b * P:(b + 1) * P], glo[s % 2][:, b * P:(b + 1) * P]
                        for st, mv in ((wh, vh), (wh, vl), (wl, vh)):
                            for q in range(2):
                                last = pe.matmul(acc[b][q][:], st, mv[:, q * 512:(q + 1) * 512], start=False, stop=False)
                    last.then_inc(tile_done, 1)
            for b in range(TB):
                for q in range(2):
                    last = pe.matmul(acc[b][q][:], zero[:, 0:P], zero[:], start=False, stop=True)
            last.then_inc(acc_done, 1)


def constants():
    c = np.zeros((P, N_CONST), np.float32)

    def put(name, a):
        c[:, CONST[name][0]:CONST[name][1]] = a

    put("ident", np.eye(P, dtype=np.float32))
    put("iota", np.arange(P, dtype=np.float32)[None, :])
    put("ones", 1.0)
    put("iota16", np.arange(16, dtype=np.float32)[None, :])
    rope = DH // 4
    half = rope // 2
    inv = (np.float32(500000.0) ** (-np.arange(0, rope, 2, dtype=np.float32) / np.float32(rope))).astype(np.float32)
    ang = (np.arange(T, dtype=np.float32)[:, None] * inv[None, :]).astype(np.float32)
    rot = np.zeros((P, P), np.float32)
    cos = np.ones((P, T), np.float32)
    sin = np.zeros((P, T), np.float32)
    for m in range(2):
        for d in range(rope):
            p = m * DH + d
            rot[m * DH + (d + half) % rope, p] = 1.0
            cos[p] = np.cos(ang[:, d % half])
            sin[p] = np.sin(ang[:, d % half]) * (-1.0 if d < half else 1.0)
    put("rot", rot)
    put("cos", cos)
    put("sin", sin)
    colq = np.arange(P) % GRID_W
    start = np.clip(colq - KC // 2, 0, GRID_W - KC)
    ck = np.arange(GRID_W)
    put("mask", np.where((ck[None, :] >= start[:, None]) & (ck[None, :] < start[:, None] + KC), 0.0, MASKED).astype(np.float32))
    return c


def kernel(x, w_in, w_proj_a, w_proj_b, w_out, norm_mix, norm_ffn, norm_final,
           lambda_q1, lambda_k1, lambda_q2, lambda_k2, diff_subln, na_rpb,
           peer_w_query, peer_sub_keys, peer_u, peer_v):
    import concourse.bacc as bacc
    from concourse.bass_utils import run_bass_kernel_spmd

    def tiles(w):
        w = np.asarray(w)
        return w.reshape(C, P, -1, P).transpose(2, 1, 0, 3)

    w_proj = np.concatenate([np.asarray(w_proj_a)[0], np.asarray(w_proj_b)[0]], axis=0)
    stream = np.concatenate([tiles(np.asarray(w_in)[0]), tiles(w_proj), tiles(np.asarray(w_out)[0]),
                             tiles(np.asarray(peer_w_query)[0]), tiles(np.asarray(peer_u)[0].T)], axis=0)
    vrows = np.asarray(peer_v)[0].reshape(NE_TILES, P, C, P)
    xT = np.asarray(x)[0].T.reshape(C, P, T).transpose(1, 0, 2)
    cols = np.concatenate([np.asarray(norm_mix)[0].reshape(C, P).T, np.asarray(norm_ffn)[0].reshape(C, P).T,
                           np.asarray(diff_subln)[0].reshape(P, 1)], axis=1)
    keys = np.asarray(peer_sub_keys)[0].reshape(HP, NK, P).transpose(2, 0, 1)
    tok = np.arange(T)
    dr = tok[None, :] // GRID_W - tok[:, None] // GRID_W + KR_MAX - 1
    dc = np.clip(tok[None, :] % GRID_W - tok[:, None] % GRID_W + KC - 1, 0, 2 * KC - 2)
    bias = np.asarray(na_rpb)[0][:, dr, dc].reshape(HB, TB, P, T).transpose(2, 1, 0, 3)
    lamv = np.concatenate([np.asarray(v) for v in (lambda_q1, lambda_k1, lambda_q2, lambda_k2)], axis=0)

    nc = bacc.Bacc("TRN2", target_bir_lowering=False, num_devices=1)
    arrays, aps = {}, {}
    for name, a in (("stream", stream), ("vrows", vrows), ("xTin", xT), ("consts", constants()), ("cols", cols),
                    ("keys", keys), ("bias", bias), ("lamv", lamv), ("gfin", np.asarray(norm_final).reshape(1, D))):
        a = np.ascontiguousarray(a)
        arrays[f"in_{name}"] = a
        aps[name] = nc.dram_tensor(f"in_{name}", a.shape, mybir.dt.from_np(a.dtype), kind="ExternalInput").ap()
    h1_dram = nc.dram_tensor("h1_scratch", (P, TB, D), F32).ap()
    a_dram = nc.dram_tensor("a_scratch", (NE_TILES, P, T), F32).ap()
    out = nc.dram_tensor("out_0", (P, TB, D), F32, kind="ExternalOutput").ap()
    build(nc, aps["stream"], aps["vrows"], {"xT": aps["xTin"], "cst": aps["consts"]}, aps["cols"], aps["keys"], aps["bias"],
          aps["lamv"], aps["gfin"], h1_dram, a_dram, out)
    r = run_bass_kernel_spmd(nc, [arrays], core_ids=[0])
    y = np.asarray(r.results[0]["out_0"])
    return y.transpose(1, 0, 2).reshape(1, T, D)
```

```python
from contextlib import ExitStack

import numpy as np

import concourse.bass as bass
from concourse import mybir

F32 = mybir.dt.float32
F32R = mybir.dt.float32r
BF16 = mybir.dt.bfloat16
U32 = mybir.dt.uint32
ALU = mybir.AluOpType
ACT = mybir.ActivationFunctionType
AX_X = mybir.AxisListType.X

P = 128
T = 256
TB = T // P
D = 1024
C = D // P
DH = 64
HA = 4
HB = 8
GRID_W, KC, KR_MAX = 64, 16, 8
ROWS = T // GRID_W
PH, NK, TOPK = 8, 128, 16
HP = PH * 2
EPS = 1e-6
LAM_INIT = 0.8 - 0.6 * float(np.exp(-0.0))
SCALE = DH ** -0.5
SINK = -3.0e38
MASKED = -1.0e30

T_QA, T_KA, T_VA = 0, HA, 2 * HA
T_QB = 3 * HA
T_KB, T_VB = T_QB + 4, T_QB + 8
T_GATE = T_QB + 12
T_PROJ = T_GATE + 16
T_OUT = T_PROJ + C
T_QUERY = T_OUT + C
T_U = T_QUERY + HP
NE_TILES = NK
T_V = T_U + NE_TILES
T_END = T_V + NE_TILES
RAW = 4
RING = 4
LEAD = 3

UNITS_A, UNITS_B = 8, 8
SLOT_A, SLOT_B = T_QB, T_GATE
G_FIRST = 60
GTOK = 4
G_STEPS = T // GTOK
G_END = G_FIRST + G_STEPS

CONST = {}
_at = 0
for _name, _n in (("rot", P), ("cos", T), ("sin", T), ("iota16", 16), ("mask", GRID_W)):
    CONST[_name] = (_at, _at + _n)
    _at += _n
N_CONST = _at


def unit_slot(n):
    return SLOT_A + n if n < UNITS_A else SLOT_B + n - UNITS_A


def units_at(slot, lag):
    return [n for n in range(UNITS_A + UNITS_B) if unit_slot(n) + lag == slot]


def token_pair(t):
    return T_VA <= t < T_QB or T_VB <= t < T_GATE


def bank_of(t):
    return (t // 2) % 2 if token_pair(t) else t % 2


def last_use(t):
    return max((x for x in range(t) if bank_of(x) == bank_of(t)), default=None)


def evac_engine(t):
    dve = lambda x: x < T_VA or T_PROJ <= x < T_U
    same = [x for x in range(t + 1) if dve(x) == dve(t)]
    return dve(t), len(same)


def act_takings(t):
    return sum(not evac_engine(x)[0] for x in range(t))


def build(nc, stream, vrows, const, cols, keys, bias, lamv, gfin, h1_dram, a_dram, out):
    with ExitStack() as top:
        def psum(name, shape):
            return top.enter_context(nc.psum_tensor(name, shape, F32))

        def sem(name):
            return top.enter_context(nc.semaphore(name))

        def sbs(stack, name, shape, dt=F32):
            return stack.enter_context(nc.sbuf_tensor(name, shape, dt))

        raw = [sbs(top, f"raw{s}", [P, C, P]) for s in range(RAW)]
        whis = sbs(top, "whis", [P, RING, C, P], F32R)
        wlos = sbs(top, "wlos", [P, RING, C, P], F32R)
        whi = [whis[:, s] for s in range(RING)]
        wlo = [wlos[:, s] for s in range(RING)]
        with ExitStack() as front:
            cst = sbs(front, "cst", [P, N_CONST])
            col = sbs(front, "col", [P, 2 * C + 1])
            xT = sbs(front, "xT", [P, C, T])
            rstd = sbs(front, "rstd", [P, T])
            ones = sbs(front, "ones", [P, P])
            with ExitStack() as mixer:
                qkT = sbs(mixer, "qkT", [P, 16, T])
                gates = sbs(mixer, "gates", [P, 16, T])
                vtok = sbs(mixer, "vtok", [P, TB, 8, P])
                biasm = sbs(mixer, "biasm", [P, TB, HB, T])
                prob = sbs(mixer, "prob", [P, 2, 2, T])
                dif = sbs(mixer, "dif", [P, 2, T])
                probT = sbs(mixer, "probT", [P, 2, 2 * T])
                rtmp = sbs(mixer, "rtmp", [P, 2, T])
                oA = sbs(mixer, "oA", [P, TB, HA, P])
                oB = sbs(mixer, "oB", [P, TB, HA, P])
                yf = sbs(mixer, "yf", [P, HA, P])
                mtmp = sbs(mixer, "mtmp", [P, 2, T])
                mfull = sbs(mixer, "mfull", [P, 2, T])
                mhi = sbs(mixer, "mhi", [P, C, T], F32R)
                mlo = sbs(mixer, "mlo", [P, C, T], F32R)
                yhi = sbs(mixer, "yhi", [P, C, T], F32R)
                ylo = sbs(mixer, "ylo", [P, C, T], F32R)
            with ExitStack() as router:
                qp = sbs(router, "qp", [P, HP, T])
                qpad = sbs(router, "qpad", [P, 16, T])
                keysT = sbs(router, "keysT", [P, HP, NK])
                sc = sbs(router, "sc", [P, TB, HP, NK])
                scm = sbs(router, "scm", [P, NK])
                top_v = sbs(router, "top_v", [P, TB, HP, TOPK])
                top_i = sbs(router, "top_i", [P, TB, HP, TOPK], U32)
                top_f = sbs(router, "top_f", [P, TB, HP, TOPK])
                cand = sbs(router, "cand", [P, PH, TOPK * TOPK])
                candm = sbs(router, "candm", [P, TOPK * TOPK])
                pick_v = sbs(router, "pick_v", [P, PH, TOPK])
                pick_p = sbs(router, "pick_p", [P, PH, TOPK], U32)
                pick_h = sbs(router, "pick_h", [P, 2, PH, TOPK], U32)
                pick_f = sbs(router, "pick_f", [P, 2, PH, TOPK])
                eq = sbs(router, "eq", [P, PH * TOPK, TOPK])
                route = sbs(router, "route", [P, TB, 3, PH, TOPK])
                gsum = sbs(router, "gsum", [P, 2, PH])
                h1tok = sbs(router, "h1tok", [P, TB, D])
        G = sbs(top, "G", [P, NK, T])
        mx = sbs(top, "mx", [P, 16, 2])
        nmx = sbs(top, "nmx", [P, 16, 2])
        zs = sbs(top, "zs", [P, 16, 2])
        rz = sbs(top, "rz", [P, 16, 2])
        lam = sbs(top, "lam", [P, 8])
        fin = sbs(top, "fin", [P, 8])
        ssA = sbs(top, "ssA", [P, 2, TB * HA])
        idio = sbs(top, "idio", [P, 2, P])
        ident, iota = idio[:, 0, :], idio[:, 1, :]
        with ExitStack() as uphase:
            xhi = sbs(uphase, "xhi", [P, C, T], F32R)
            xlo = sbs(uphase, "xlo", [P, C, T], F32R)
            routeT = sbs(uphase, "routeT", [P, 3, T])
            onehot = [sbs(uphase, f"onehot{s}", [P, 2, GTOK, P]) for s in range(2)]
            ast = [sbs(uphase, f"ast{s}", [P, T]) for s in range(2)]
        with ExitStack() as vphase:
            htok = sbs(vphase, "htok", [P, TB, D])
            gf = sbs(vphase, "gf", [P, D])
            fsq = sbs(vphase, "fsq", [P, D])
            glo = [sbs(vphase, f"glo{s}", [P, T], F32R) for s in range(2)]
            vpad = sbs(vphase, "vpad", [P, T])
            aring = [sbs(vphase, f"aring{s}", [P, T]) for s in range(4)]
            wfull = [sbs(vphase, f"wfull{s}", [P, T]) for s in range(2)]
            ghi = [sbs(vphase, f"ghi{s}", [P, T], F32R) for s in range(2)]

        def K(name):
            a, b = CONST[name]
            return cst[:, a:b]

        pO = [psum("pO0", [P, 512]), psum("pO1", [P, 512])]
        pSS = psum("pSS", [P, 2, 512])
        pS = [pSS[:, 0, :], pSS[:, 1, :]]
        pT = [psum("pT0", [P, 512]), psum("pT1", [P, 512])]
        pM = [psum("pM0", [P, 512]), psum("pM1", [P, 512])]
        acc = [[pT[0], pT[1]], [pM[0], pM[1]]]

        raw_landed = [sem(f"raw_landed{s}") for s in range(RAW)]
        x_landed = [sem("x_landed0"), sem("x_landed1")]
        gains_landed = sem("gains_landed")
        const_landed = sem("const_landed")
        ones_ready = sem("ones_ready")
        squares_dve = sem("squares_dve")
        bias_landed = sem("bias_landed")
        keys_landed = sem("keys_landed")
        hi_ready = sem("hi_ready")
        lo_ready = sem("lo_ready")
        tile_done = sem("tile_done")
        evac_act = sem("evac_act")
        evac_dve = sem("evac_dve")
        dve_order = sem("dve_order")
        squares = sem("squares")
        ssq_done = sem("ssq_done")
        meansq = sem("meansq")
        root = sem("root")
        normed = sem("normed")
        norm_hi = sem("norm_hi")
        norm_lo = sem("norm_lo")
        lam_sums = sem("lam_sums")
        lam_exps = sem("lam_exps")
        gain_hi = sem("gain_hi")
        gain_lo = sem("gain_lo")
        rot_done = sem("rot_done")
        roped = sem("roped")
        bias_masked = sem("bias_masked")
        scores_done = sem("scores_done")
        scores_taken = sem("scores_taken")
        max_ready = sem("max_ready")
        exp_done = sem("exp_done")
        dif_ready = sem("dif_ready")
        probs_turned = sem("probs_turned")
        turned_taken = sem("turned_taken")
        pv_done = sem("pv_done")
        pv_taken = sem("pv_taken")
        ya_meansq = sem("ya_meansq")
        ya_root = sem("ya_root")
        y_ready = sem("y_ready")
        y_turned = sem("y_turned")
        y_full = sem("y_full")
        y_hi = sem("y_hi")
        y_lo = sem("y_lo")
        m_full = sem("m_full")
        m_hi = sem("m_hi")
        m_lo = sem("m_lo")
        h1_turned = sem("h1_turned")
        h1_taken = sem("h1_taken")
        h1_stored = sem("h1_stored")
        key_scores = sem("key_scores")
        sbank_taken = sem("sbank_taken")
        pick_max = sem("pick_max")
        pick_exp = sem("pick_exp")
        routed = sem("routed")
        route_turned = sem("route_turned")
        route_taken = sem("route_taken")
        onehot_ready = sem("onehot_ready")
        g_done = sem("g_done")
        gelu_done = sem("gelu_done")
        a_stored = [sem(f"a_stored{s}") for s in range(2)]
        a_landed = [sem(f"a_landed{s}") for s in range(4)]
        final_landed = sem("final_landed")
        w_ready = sem("w_ready")
        ghi_ready = sem("ghi_ready")
        glo_ready = sem("glo_ready")
        vlo_ready = sem("vlo_ready")
        acc_done = sem("acc_done")
        h2_ready = sem("h2_ready")
        fin_sum = sem("fin_sum")
        fin_ms = sem("fin_ms")
        fin_root = sem("fin_root")
        out_ready = sem("out_ready")
        out_stored = sem("out_stored")

        block = top.enter_context(nc.Block())

        @block.sync
        def _(sp):
            half = C // 2
            sp.dma_start(raw[0][:], stream[0]).then_inc(raw_landed[0], 16)
            sp.dma_start(col[:], cols).then_inc(gains_landed, 16)
            for q in range(2):
                sp.dma_start(xT[:, q * half:(q + 1) * half, :], const["xT"][:, q * half:(q + 1) * half, :]).then_inc(x_landed[q], 16)
            sp.dma_start(raw[1][:], stream[1]).then_inc(raw_landed[1], 16)
            sp.dma_start(rtmp[:, :, 0:2 * DH], lamv.to_broadcast([P, 2, 2 * DH])).then_inc(const_landed, 16)
            sp.dma_start(cst[:], const["cst"]).then_inc(const_landed, 16)
            for t in range(2, RAW):
                sp.dma_start(raw[t][:], stream[t]).then_inc(raw_landed[t], 16)
            sp.dma_start(idio[:], const["idio"]).then_inc(const_landed, 16)

            def load(t, s, row):
                sp.wait_ge(lo_ready, t - RAW + 1)
                sp.dma_start(raw[s][:], row).then_inc(raw_landed[s], 16)

            for t in range(RAW, 2 * RAW):
                load(t, t % RAW, stream[t])
            sp.dma_start(biasm[:], bias).then_inc(bias_landed, 16)
            with sp.Fori(2, T_QUERY // RAW + 1) as g:
                for s in range(RAW):
                    load(g * RAW + s, s, stream[bass.ds(g * RAW + s, 1)])
            sp.wait_ge(tile_done, T_OUT)
            sp.dma_start(keysT[:], keys).then_inc(keys_landed, 16)
            with sp.Fori(T_QUERY // RAW + 1, T_U // RAW) as g:
                for s in range(RAW):
                    load(g * RAW + s, s, stream[bass.ds(g * RAW + s, 1)])
            sp.wait_ge(h1_taken, 4)
            sp.dma_start(h1_dram, h1tok[:]).then_inc(h1_stored, 16)
            with sp.Fori(T_U // RAW, T_V // RAW) as g:
                for s in range(RAW):
                    load(g * RAW + s, s, stream[bass.ds(g * RAW + s, 1)])
            for s in range(RAW):
                load(T_V + s, s, vrows[s:s + 1])
            for s in range(2):
                sp.wait_ge(a_stored[s], 16 * (NE_TILES // 2))
            lower, upper = slice(0, C // 2), slice(C // 2, C)

            def load_v(i, s):
                row = vrows[i] if isinstance(i, int) else vrows[bass.ds(i, 1)].rearrange("o p c n -> (o p) c n")
                sp.wait_ge(lo_ready, i + (T_V - RAW + 1))
                sp.dma_start(raw[s][:, lower, :], row[:, lower, :]).then_inc(raw_landed[s], 16)
                sp.wait_ge(vlo_ready, i - RAW + 1)
                sp.dma_start(raw[s][:, upper, :], row[:, upper, :]).then_inc(raw_landed[s], 16)
                sp.wait_ge(w_ready, i - 3)
                sp.dma_start(aring[s][:], a_dram[bass.ds(i, 1)] if not isinstance(i, int) else a_dram[i]).then_inc(a_landed[s], 16)

            for s in range(RAW):
                load_v(RAW + s, s)
            sp.wait_ge(tile_done, T_V)
            sp.wait_ge(h1_stored, 16)
            sp.dma_start(gf[:], gfin.to_broadcast([P, D])).then_inc(final_landed, 16)
            sp.dma_start(htok[:], h1_dram).then_inc(final_landed, 16)
            with sp.Fori(2, NE_TILES // RAW) as g:
                for s in range(RAW):
                    load_v(g * RAW + s, s)
            for b in range(TB):
                sp.wait_ge(out_ready, b + 1)
                sp.dma_start(out[:, b, :], htok[:, b, :]).then_inc(out_stored, 16)
            sp.wait_ge(out_stored, 16 * TB)

        @block.gpsimd
        def _(pool):
            pool.memset(ones[:], 1.0).then_inc(ones_ready, 1)

            def low(t, s):
                pool.wait_ge(hi_ready, t + 1)
                pool.tensor_tensor(wlo[s], raw[s][:], whi[s].bitcast(F32), ALU.subtract).then_inc(lo_ready, 1)

            for t in range(2 * RING):
                low(t, t % RING)
            pool.wait_ge(bias_landed, 16)
            pool.wait_ge(const_landed, 16 * 3)
            bview = biasm[:].rearrange("p b h (r c) -> p b (h r) c", c=GRID_W)
            mask = K("mask").unsqueeze(1).to_broadcast([P, HB, GRID_W])
            for part in range(TB * ROWS):
                view = bview[:, part // ROWS, (part % ROWS) * HB:(part % ROWS + 1) * HB, :]
                pool.tensor_tensor(view, view, mask, ALU.add).then_inc(bias_masked, 1)
                low(2 * RING + part, part % RING)
            with pool.Fori(4, T_V // RING) as g:
                for s in range(RING):
                    low(g * RING + s, s)
            with pool.Fori(T_V // RING, T_END // RING) as g:
                for s in range(RING):
                    pool.wait_ge(hi_ready, g * RING + s + 1)
                    pool.tensor_tensor(wlo[s][:, 0:C // 2, :], raw[s][:, 0:C // 2, :], whi[s][:, 0:C // 2, :].bitcast(F32),
                                       ALU.subtract).then_inc(lo_ready, 1)

        @block.scalar
        def _(act):
            def hi(t, s, turn):
                act.wait_ge(raw_landed[s], turn * 16)
                if not (isinstance(t, int) and t < RING):
                    act.wait_ge(tile_done, t - RING + 1)
                act.activation(whi[s], raw[s][:], ACT.Copy).then_inc(hi_ready, 1)

            def landings(t):
                return t // RAW + 1 + max(0, t // RAW - T_V // RAW)

            def hi_at(t):
                if t < T_END:
                    hi(t, t % RING, landings(t))

            def gained_hi(gain0, c):
                act.activation(yhi[:, c, :], xT[:, c, :], ACT.Copy, scale=col[:, gain0 + c:gain0 + c + 1]).then_inc(gain_hi, 1)

            def rms_root(k):
                act.wait_ge(meansq, k)
                act.activation(rstd[:], rstd[:], ACT.Sqrt).then_inc(root, 1)

            def normed_hi(k, c):
                act.wait_ge(normed, C * (k - 1) + c + 1)
                act.activation(xhi[:, c, :], gates[:, c, :], ACT.Copy).then_inc(norm_hi, 1)

            act.preload_act_table(ACT.Sqrt)
            hi_at(0)
            act.wait_ge(gains_landed, 16)
            for c in range(C):
                act.wait_ge(x_landed[c // (C // 2)], 16)
                gained_hi(0, c)
            hi_at(1)
            act.activation(gates[:, 0:C // 2, :], xT[:, 0:C // 2, :], ACT.Square).then_inc(squares, 1)
            hi_at(2)
            rms_root(1)
            act.wait_ge(lam_sums, 1)
            act.activation(lam[:, 2:4], lam[:, 0:2], ACT.Exp).then_inc(lam_exps, 1)
            for k in range(T_PROJ):
                hi_at(k + LEAD)
                if k < C:
                    normed_hi(1, k)
                if token_pair(k):
                    if k % 2:
                        act.wait_ge(tile_done, k + 1)
                        v = k - 1 - T_VA if k < T_QB else k - 1 - T_VB + HA
                        act.activation(vtok[:, :, v:v + 2, :], pO[bank_of(k)][:].rearrange("p (b v n) -> p b v n", b=TB, v=2),
                                       ACT.Copy).then_inc(evac_act, 2)
                elif k >= T_VA:
                    act.wait_ge(tile_done, k + 1)
                    src = pO[bank_of(k)][:, 0:T]
                    if k >= T_GATE:
                        act.activation(gates[:, k - T_GATE, :], src, ACT.Tanh, scale=0.5).then_inc(evac_act, 1)
                    else:
                        act.activation(qkT[:, k - T_QB + 8, :], src, ACT.Copy).then_inc(evac_act, 1)
                for n in units_at(k, 0):
                    act.wait_ge(max_ready, n + 1)
                    if n >= 2:
                        if n - 2 < UNITS_A:
                            act.wait_ge(dif_ready, n - 1)
                        else:
                            act.wait_ge(probs_turned, n - 1)
                    for m in range(2):
                        src, scale = (pS[m][:, 0:T], SCALE) if n < UNITS_A else (prob[:, n % 2, m, :], 1.0)
                        act.activation(prob[:, n % 2, m, :], src, ACT.Exp, bias=nmx[:, n, m:m + 1], scale=scale,
                                       accum_out=zs[:, n, m:m + 1]).then_inc(exp_done, 1)
                if k == T_GATE - 1:
                    act.wait_ge(ya_meansq, 1)
                    act.activation(ssA[:, 0, :], ssA[:, 0, :], ACT.Sqrt).then_inc(ya_root, 1)
                if k in (T_GATE, T_GATE + 1, T_PROJ - 3, T_PROJ - 2):
                    j = {T_GATE: 0, T_GATE + 1: 1, T_PROJ - 3: 2, T_PROJ - 2: 3}[k]
                    act.wait_ge(y_full, j + 1)
                    half, b = j // 2, j % 2
                    act.activation(yhi[:, half * HA:(half + 1) * HA, b * P:(b + 1) * P], yf[:], ACT.Copy).then_inc(y_hi, 1)
            for k in range(T_PROJ, T_QUERY):
                hi_at(k + LEAD)
                if k < T_OUT:
                    j = k - T_PROJ
                    act.wait_ge(m_full, j + 1)
                    act.activation(mhi[:, j, :], mfull[:, j % 2, :], ACT.Copy).then_inc(m_hi, 1)
                elif k == T_OUT:
                    act.preload_act_table(ACT.Sqrt)
                if k >= T_OUT:
                    act.wait_ge(evac_dve, evac_engine(k)[1])
                    gained_hi(C, k - T_OUT)
                    act.activation(gates[:, k - T_OUT, :], xT[:, k - T_OUT, :], ACT.Square).then_inc(squares, 1)
            for k in range(T_QUERY, T_U):
                hi_at(k + LEAD)
                if k == T_QUERY:
                    rms_root(2)
                if k - T_QUERY < C:
                    normed_hi(2, k - T_QUERY)
            act.preload_act_table(ACT.Gelu)

            def gelu(t, i, s2, turns):
                act.wait_ge(tile_done, t + 1)
                if turns is not None:
                    act.wait_ge(a_stored[s2], turns)
                act.activation(ast[s2][:], pO[s2][:, 0:T], ACT.Gelu).then_inc(evac_act, 1)

            def store(i, s2, count):
                act.wait_ge(evac_act, count)
                act.dma_start(a_dram[bass.ds(i, 1)] if not isinstance(i, int) else a_dram[i], ast[s2][:]).then_inc(a_stored[s2], 16)

            base = act_takings(T_U)

            for i in range(8):
                hi_at(T_U + i + LEAD)
                n = i
                act.wait_ge(key_scores, n + 1)
                b, q4 = n // 4, n % 4
                act.activation(sc[:, b, q4 * 4:(q4 + 1) * 4, :], pS[n % 2].rearrange("p (h k) -> p h k", h=4), ACT.Copy).then_inc(sbank_taken, 1)
                gelu(T_U + i, i, i % 2, None if i < 2 else 16 * (i // 2))
                store(i, i % 2, base + i + 1)
            def u_step(g, s):
                i = g * 4 + s
                hi(i + (T_U + LEAD), (s + LEAD) % RING, g + (T_U // RAW + (s + LEAD) // RAW + 1))
                gelu(i + T_U, i, s % 2, (g * 2 + s // 2) * 16)
                store(i, s % 2, i + (base + 1))
                return i

            for b, (i0, stop) in enumerate(((8, 20), (20, 40))):
                with act.Fori(i0 // 4, stop // 4) as g:
                    for s in range(4):
                        u_step(g, s)
                act.wait_ge(pick_max, b + 1)
                act.activation(route[:, b, 2, :, :], route[:, b, 2, :, :], ACT.Exp).then_inc(pick_exp, 1)
                act.preload_act_table(ACT.Gelu)
            with act.Fori(40 // 4, G_FIRST // 4) as g:
                for s in range(4):
                    u_step(g, s)
            with act.Fori(G_FIRST // 4, G_END // 4) as g:
                for s in range(4):
                    i = u_step(g, s)
                    act.wait_ge(g_done, i - G_FIRST + 1)
                    act.activation(G[:, :, bass.ds((i - G_FIRST) * GTOK, GTOK)].rearrange("p i t -> p t i"),
                                   pS[s % 2].rearrange("p (t i) -> p t i", t=GTOK), ACT.Copy).then_inc(sbank_taken, 1)
            for s in range(4):
                act.wait_ge(a_stored[s % 2], 16 * (s // 2 + 1))
                act.dma_start(aring[s][:], a_dram[s]).then_inc(a_landed[s], 16)
            with act.Fori(G_END // 4, NE_TILES // 4) as g:
                for s in range(4):
                    u_step(g, s)
            act.preload_act_table(ACT.Sqrt)

            def w_hi(i, s):
                act.wait_ge(w_ready, i + 1)
                act.wait_ge(tile_done, i + (T_V - 1))
                act.activation(ghi[s % 2][:], wfull[s % 2][:], ACT.Copy).then_inc(ghi_ready, 1)

            with act.Fori(0, NE_TILES // 4 - 1) as g:
                for s in range(4):
                    w_hi(g * 4 + s, s)
                    hi(g * 4 + (s + T_V + LEAD), (s + LEAD) % RING, g * 2 + landings(T_V + s + LEAD))
            for i in range(NE_TILES - 4, NE_TILES):
                w_hi(i, i)
                hi_at(T_V + i + LEAD)
            for b in range(TB):
                act.wait_ge(h2_ready, 2 * (b + 1))
                if b:
                    act.wait_ge(fin_sum, b)
                act.activation(fsq[:], htok[:, b, :], ACT.Square, accum_out=fin[:, b:b + 1]).then_inc(fin_sum, 1)
            for b in range(TB):
                act.wait_ge(fin_ms, b + 1)
                act.activation(fin[:, 4 + b:5 + b], fin[:, 2 + b:3 + b], ACT.Sqrt).then_inc(fin_root, 1)

        @block.vector
        def _(dve):
            order = [0]

            def link(ins):
                order[0] += 1
                ins.then_inc(dve_order, 1)
                dve.wait_ge(dve_order, order[0])

            def gained_low(gain0, c):
                done = (C if gain0 else 0) + c + 1
                dve.wait_ge(gain_hi, done)
                dve.scalar_tensor_tensor(ylo[:, c, :], xT[:, c, :], col[:, gain0 + c:gain0 + c + 1], yhi[:, c, :].bitcast(F32),
                                         ALU.mult, ALU.subtract).then_inc(gain_lo, 1)

            def rms(k):
                dve.wait_ge(ssq_done, k)
                dve.tensor_scalar(rstd[:], pM[0][:, 0:T], 1.0 / D, EPS, ALU.mult, ALU.add).then_inc(meansq, 1)
                dve.wait_ge(root, k)
                link(dve.reciprocal(rstd[:], rstd[:]))

            def normed_full(k, gain0, c):
                dve.scalar_tensor_tensor(gates[:, c, :], xT[:, c, :], col[:, gain0 + c:gain0 + c + 1], rstd[:],
                                         ALU.mult, ALU.mult).then_inc(normed, 1)

            def normed_low(k, c):
                done = C * (k - 1) + c + 1
                dve.wait_ge(normed, done)
                dve.wait_ge(norm_hi, done)
                dve.tensor_tensor(xlo[:, c, :], gates[:, c, :], xhi[:, c, :].bitcast(F32), ALU.subtract).then_inc(norm_lo, 1)

            dve.wait_ge(gains_landed, 16)
            for c in range(C):
                dve.wait_ge(x_landed[c // (C // 2)], 16)
                gained_low(0, c)
            dve.tensor_tensor(gates[:, C // 2:C, :], xT[:, C // 2:C, :], xT[:, C // 2:C, :], ALU.mult).then_inc(squares_dve, 1)
            dve.wait_ge(const_landed, 16 * 3)
            for m in range(2):
                link(dve.tensor_tensor(mtmp[:, m, 0:DH], rtmp[:, m, 0:DH], rtmp[:, m, DH:2 * DH], ALU.mult))
            dve.tensor_reduce(lam[:, 0:2], mtmp[:, :, 0:DH], AX_X, ALU.add).then_inc(lam_sums, 1)
            rms(1)

            def lambda_rest():
                dve.wait_ge(lam_exps, 1)
                link(dve.tensor_tensor(lam[:, 4:5], lam[:, 3:4], lam[:, 2:3], ALU.subtract))
                link(dve.tensor_scalar(lam[:, 5:6], lam[:, 4:5], -LAM_INIT, None, ALU.add))
                link(dve.tensor_scalar(lam[:, 6:7], col[:, 2 * C:2 * C + 1], 1.0 - LAM_INIT, None, ALU.mult))

            def take_turned(n):
                if n >= 2:
                    dve.wait_ge(pv_done, n - 1)
                dve.wait_ge(probs_turned, n + 1)
                w = T if n < UNITS_A else 2 * T
                dve.tensor_copy(probT[:, n % 2, 0:w], pT[n % 2][:, 0:w]).then_inc(turned_taken, 1)

            def take_pv(n):
                dve.wait_ge(pv_done, n + 1)
                if n < UNITS_A:
                    h, b = n % HA, n // HA
                    dve.tensor_copy(oA[:, b, h, :], pM[n % 2][:, 0:P]).then_inc(pv_taken, 1)
                else:
                    h, b = (n - UNITS_A) % HA, (n - UNITS_A) // HA
                    dve.tensor_tensor(oB[:, b, h, :].rearrange("p (m v) -> p m v", m=2),
                                      pM[n % 2][:, 0:P].rearrange("p (m v) -> p m v", m=2),
                                      rz[:, n, :].unsqueeze(2).to_broadcast([P, 2, DH]), ALU.mult).then_inc(pv_taken, 1)

            def y_parts(j):
                half, b = j // 2, j % 2
                dve.wait_ge(y_turned, j + 1)
                if j:
                    dve.wait_ge(y_lo, j)
                src = pT[j % 2][:].rearrange("p (h t) -> p h t", h=HA)
                if half == 0:
                    dve.tensor_scalar(yf[:], src, lam[:, 6:7], None, ALU.mult).then_inc(y_full, 1)
                else:
                    dve.tensor_copy(yf[:], src).then_inc(y_full, 1)
                dve.wait_ge(y_full, j + 1)
                dve.wait_ge(y_hi, j + 1)
                at = (slice(None), slice(half * HA, (half + 1) * HA), slice(b * P, (b + 1) * P))
                dve.tensor_tensor(ylo[at], yf[:], yhi[at].bitcast(F32), ALU.subtract).then_inc(y_lo, 1)

            for k in range(T_PROJ + 1):
                if k < T_VA:
                    dve.wait_ge(tile_done, k + 1)
                    dve.tensor_tensor(qkT[:, k, :], pO[k % 2][:, 0:T], rstd[:], ALU.mult).then_inc(evac_dve, 1)
                    normed_full(1, 0, k)
                    dve.wait_ge(evac_dve, k + 1)
                    link(dve.tensor_tensor(rtmp[:, 0, :], qkT[:, k, :], K("cos"), ALU.mult))
                    normed_low(1, k)
                    dve.wait_ge(rot_done, k + 1)
                    link(dve.tensor_tensor(rtmp[:, 1, :], pM[k % 2][:, 0:T], K("sin"), ALU.mult))
                    dve.tensor_tensor(qkT[:, k, :], rtmp[:, 0, :], rtmp[:, 1, :], ALU.add).then_inc(roped, 1)
                    dve.wait_ge(roped, k + 1)
                    if k == 0:
                        lambda_rest()
                for n in units_at(k, 1):
                    dve.wait_ge(exp_done, 2 * (n + 1))
                    if n < UNITS_A:
                        link(dve.reciprocal(rz[:, n, :], zs[:, n, :]))
                        link(dve.tensor_tensor(rz[:, n, 1:2], rz[:, n, 1:2], lam[:, 5:6], ALU.mult))
                        if n >= 2:
                            dve.wait_ge(probs_turned, n - 1)
                        link(dve.tensor_scalar(rtmp[:, 0, :], prob[:, n % 2, 1, :], rz[:, n, 1:2], None, ALU.mult))
                        dve.scalar_tensor_tensor(dif[:, n % 2, :], prob[:, n % 2, 0, :], rz[:, n, 0:1], rtmp[:, 0, :],
                                                 ALU.mult, ALU.add).then_inc(dif_ready, 1)
                        dve.wait_ge(dif_ready, n + 1)
                    else:
                        link(dve.reciprocal(rz[:, n, :], zs[:, n, :]))
                for n in units_at(k, 0):
                    dve.wait_ge(scores_done, n + 1)
                    if n < UNITS_A:
                        link(dve.tensor_reduce(mx[:, n, :], pSS[:, :, 0:T], AX_X, ALU.max))
                        dve.tensor_scalar(nmx[:, n, :], mx[:, n, :], -SCALE, None, ALU.mult).then_inc(max_ready, 1)
                    else:
                        h, b = (n - UNITS_A) % HA, (n - UNITS_A) // HA
                        if n == UNITS_A:
                            dve.wait_ge(bias_masked, TB * ROWS)
                        if n - 2 >= UNITS_A:
                            dve.wait_ge(probs_turned, n - 1)
                        dve.scalar_tensor_tensor(prob[:, n % 2, :, :], pSS[:, :, 0:T], SCALE,
                                                 biasm[:, b, 2 * h:2 * h + 2, :], ALU.mult, ALU.add).then_inc(scores_taken, 1)
                        dve.wait_ge(scores_taken, n - UNITS_A + 1)
                        link(dve.tensor_reduce(mx[:, n, :], prob[:, n % 2, :, :], AX_X, ALU.max))
                        dve.tensor_scalar(nmx[:, n, :], mx[:, n, :], -1.0, None, ALU.mult).then_inc(max_ready, 1)
                for n in units_at(k, 2):
                    take_turned(n)
                for n in units_at(k, 3):
                    take_pv(n)
                if k == T_GATE - 1:
                    dve.wait_ge(pv_taken, UNITS_A)
                    flat = oA[:].rearrange("p b h v -> p (b h) v")
                    sq = gates[:, 0:4, :].rearrange("p a b -> p (a b)").rearrange("p (u v) -> p u v", v=P)
                    link(dve.tensor_tensor(sq, flat, flat, ALU.mult))
                    link(dve.tensor_reduce(ssA[:, 1, :], sq, AX_X, ALU.add))
                    dve.tensor_scalar(ssA[:, 0, :], ssA[:, 1, :], 1.0 / P, EPS, ALU.mult, ALU.add).then_inc(ya_meansq, 1)
                    dve.wait_ge(ya_root, 1)
                    link(dve.reciprocal(ssA[:, 1, :], ssA[:, 0, :]))
                    dve.tensor_tensor(flat, flat, ssA[:, 1, :].unsqueeze(2).to_broadcast([P, TB * HA, P]), ALU.mult).then_inc(y_ready, 1)
                if k in (T_GATE, T_GATE + 1):
                    y_parts(k - T_GATE)
                if k in (T_PROJ - 3, T_PROJ - 2):
                    y_parts(k - T_PROJ + 5)
            for k in range(T_PROJ, T_OUT):
                j = k - T_PROJ
                dve.wait_ge(tile_done, k + 1)
                if j == 0:
                    dve.wait_ge(evac_act, evac_engine(T_PROJ - 1)[1])
                link(dve.scalar_tensor_tensor(mtmp[:, 0, :], gates[:, j, :], 1.0, pO[k % 2][:, 0:T], ALU.add, ALU.mult))
                dve.scalar_tensor_tensor(mtmp[:, 1, :], gates[:, C + j, :], 1.0, pO[k % 2][:, T:2 * T], ALU.add, ALU.mult).then_inc(evac_dve, 1)
                dve.wait_ge(evac_dve, evac_engine(k)[1])
                dve.tensor_tensor(mfull[:, j % 2, :], mtmp[:, 0, :], mtmp[:, 1, :], ALU.add).then_inc(m_full, 1)
                dve.wait_ge(m_full, j + 1)
                dve.wait_ge(m_hi, j + 1)
                dve.tensor_tensor(mlo[:, j, :], mfull[:, j % 2, :], mhi[:, j, :].bitcast(F32), ALU.subtract).then_inc(m_lo, 1)
                dve.wait_ge(m_lo, j + 1)
            for k in range(T_OUT, T_QUERY):
                j = k - T_OUT
                dve.wait_ge(tile_done, k + 1)
                dve.scalar_tensor_tensor(xT[:, j, :], pO[k % 2][:, 0:T], 0.5, xT[:, j, :], ALU.mult, ALU.add).then_inc(evac_dve, 1)
                dve.wait_ge(evac_dve, evac_engine(k)[1])
                gained_low(C, j)
            for k in range(T_QUERY, T_U):
                j = k - T_QUERY
                dve.wait_ge(tile_done, k + 1)
                if j == 0:
                    rms(2)
                dve.tensor_tensor(qp[:, j, :], pO[k % 2][:, 0:T], rstd[:], ALU.mult).then_inc(evac_dve, 1)
                if j < C:
                    normed_full(2, C, j)
                if 1 <= j <= 4:
                    dve.wait_ge(h1_turned, j)
                    b, q = (j - 1) // 2, (j - 1) % 2
                    dve.tensor_copy(h1tok[:, b, q * 512:(q + 1) * 512], pT[(j - 1) % 2][:]).then_inc(h1_taken, 1)
                if j < C:
                    normed_low(2, j)

            def top16(vals, idx, src, work):
                link(dve.max(vals[:, 0:8], src))
                dve.max_index(idx[:, 0:8], vals[:, 0:8], src)
                link(dve.match_replace(work, vals[:, 0:8], src, SINK))
                link(dve.max(vals[:, 8:16], work))
                link(dve.max_index(idx[:, 8:16], vals[:, 8:16], work))

            for b in range(TB):
                for h in range(HP):
                    if h % 4 == 0:
                        dve.wait_ge(sbank_taken, b * 4 + h // 4 + 1)
                    top16(top_v[:, b, h, :], top_i[:, b, h, :], sc[:, b, h, :], scm[:])
                link(dve.tensor_copy(top_f[:, b], top_i[:, b]))
                halves = top_v[:, b].rearrange("p (h q) k -> p q h k", q=2)
                for h in range(PH):
                    ins = dve.tensor_tensor(cand[:, h, :].rearrange("p (x y) -> p x y", x=TOPK),
                                            top_v[:, b, 2 * h, :].unsqueeze(2).to_broadcast([P, TOPK, TOPK]),
                                            top_v[:, b, 2 * h + 1, :].unsqueeze(1).to_broadcast([P, TOPK, TOPK]), ALU.add)
                    link(ins)
                for h in range(PH):
                    top16(pick_v[:, h, :], pick_p[:, h, :], cand[:, h, :], candm[:])
                dve.tensor_tensor(route[:, b, 2], pick_v[:], pick_v[:, :, 0:1].to_broadcast([P, PH, TOPK]), ALU.subtract).then_inc(pick_max, 1)
                link(dve.tensor_scalar(pick_h[:, 0], pick_p[:], 4, None, ALU.logical_shift_right))
                link(dve.tensor_scalar(pick_h[:, 1], pick_p[:], TOPK - 1, None, ALU.bitwise_and))
                link(dve.tensor_copy(pick_f[:], pick_h[:]))
                for q in range(2):
                    link(dve.tensor_tensor(eq[:], pick_f[:, q].rearrange("p h k -> p (h k)").unsqueeze(2).to_broadcast([P, PH * TOPK, TOPK]),
                                           K("iota16").unsqueeze(1).to_broadcast([P, PH * TOPK, TOPK]), ALU.is_equal))
                    for h in range(PH):
                        e3 = eq[:, h * TOPK:(h + 1) * TOPK, :]
                        ins = dve.tensor_tensor(e3, e3, top_f[:, b, 2 * h + q, :].unsqueeze(1).to_broadcast([P, TOPK, TOPK]), ALU.mult)
                        link(ins)
                    link(dve.tensor_reduce(route[:, b, q].rearrange("p h k -> p (h k)"), eq[:], AX_X, ALU.add))
                dve.wait_ge(pick_exp, b + 1)
                link(dve.tensor_reduce(gsum[:, 0, :], route[:, b, 2], AX_X, ALU.add))
                link(dve.reciprocal(gsum[:, 1, :], gsum[:, 0, :]))
                dve.tensor_tensor(route[:, b, 2], route[:, b, 2], gsum[:, 1, :].unsqueeze(2).to_broadcast([P, PH, TOPK]), ALU.mult).then_inc(routed, 1)
            for b in range(TB):
                dve.wait_ge(route_turned, b + 1)
                dve.tensor_copy(routeT[:, :, b * P:(b + 1) * P], pM[b][:, 0:3 * P].rearrange("p (a t) -> p a t", a=3)).then_inc(route_taken, 1)
            dve.wait_ge(route_taken, 2)

            def one_hots(k, s):
                def row(a):
                    return routeT[:, a, bass.ds(k * GTOK, GTOK)].unsqueeze(2).to_broadcast([P, GTOK, P])
                io = iota.unsqueeze(1).to_broadcast([P, GTOK, P])
                dve.tensor_tensor(onehot[s][:, 1], row(1), io, ALU.is_equal).then_inc(dve_order, 1)
                dve.tensor_tensor(onehot[s][:, 0], row(0), io, ALU.is_equal).then_inc(dve_order, 1)
                dve.wait_ge(dve_order, k * 2 + (order[0] + 2))
                dve.tensor_tensor(onehot[s][:, 1], onehot[s][:, 1], row(2), ALU.mult).then_inc(onehot_ready, 1)

            one_hots(0, 0)
            one_hots(1, 1)
            n_steps = G_STEPS
            with dve.Fori(1, n_steps // 2) as g:
                for s in range(2):
                    dve.wait_ge(g_done, g * 2 + s - 1)
                    one_hots(g * 2 + s, s)
            order[0] += 2 * n_steps

            dve.wait_ge(g_done, n_steps)
            dve.wait_ge(sbank_taken, 8 + n_steps)

            def weights(i, s, turn):
                dve.wait_ge(a_landed[s], turn * 16)
                dve.tensor_tensor(wfull[s % 2][:], aring[s][:], G[:, i, :] if isinstance(i, int) else G[:, bass.ds(i, 1), :], ALU.mult).then_inc(w_ready, 1)

            def low(i, s):
                dve.wait_ge(w_ready, i + 1)
                dve.wait_ge(ghi_ready, i + 1)
                dve.tensor_tensor(glo[s % 2][:], wfull[s % 2][:], ghi[s % 2][:].bitcast(F32), ALU.subtract).then_inc(glo_ready, 1)

            def v_low(i, s):
                dve.wait_ge(hi_ready, i + (T_V + 1))
                dve.tensor_tensor(wlo[s][:, C // 2:C, :], raw[s][:, C // 2:C, :], whi[s][:, C // 2:C, :].bitcast(F32),
                                  ALU.subtract).then_inc(vlo_ready, 1)

            weights(0, 0, 1)
            weights(1, 1, 1)
            for i in range(LEAD):
                v_low(i, i)
            with dve.Fori(0, NE_TILES // 4 - 1) as g:
                for s in range(4):
                    low(g * 4 + s, s)
                    dve.wait_ge(glo_ready, g * 4 + s + 1)
                    weights(g * 4 + s + 2, (s + 2) % 4, g + ((s + 2) // 4 + 1))
                    v_low(g * 4 + s + LEAD, (s + LEAD) % RING)
            for i in range(NE_TILES - 4, NE_TILES):
                low(i, i)
                dve.wait_ge(glo_ready, i + 1)
                if i + 2 < NE_TILES:
                    weights(i + 2, (i + 2) % 4, (i + 2) // 4 + 1)
                if i + LEAD < NE_TILES:
                    v_low(i + LEAD, (i + LEAD) % RING)

            dve.wait_ge(final_landed, 32)
            for b in range(TB):
                dve.wait_ge(acc_done, b + 1)
                for q in range(2):
                    part = htok[:, b, q * 512:(q + 1) * 512]
                    dve.tensor_tensor(part, acc[b][q][:], part, ALU.add).then_inc(h2_ready, 1)
            for b in range(TB):
                dve.wait_ge(fin_sum, b + 1)
                dve.tensor_scalar(fin[:, 2 + b:3 + b], fin[:, b:b + 1], 1.0 / D, EPS, ALU.mult, ALU.add).then_inc(fin_ms, 1)
            dve.wait_ge(h2_ready, 2 * TB)
            for b in range(TB):
                dve.wait_ge(fin_root, b + 1)
                link(dve.reciprocal(fin[:, 6 + b:7 + b], fin[:, 4 + b:5 + b]))
                dve.scalar_tensor_tensor(htok[:, b], htok[:, b], fin[:, 6 + b:7 + b], gf[:], ALU.mult, ALU.mult).then_inc(out_ready, 1)

        @block.tensor
        def _(pe):
            def split_product(dst, terms, gained=None):
                last = None
                for c, (sh, sl, mh, ml) in enumerate(terms):
                    if gained is not None:
                        pe.wait_ge(gain_lo, gained + c + 1)
                    for q, (st, mv) in enumerate(((sh, mh), (sh, ml), (sl, mh))):
                        last = pe.matmul(dst, st, mv, start=(c == 0 and q == 0), stop=(c == len(terms) - 1 and q == 2))
                return last

            def tile_wait(t):
                pe.wait_ge(lo_ready, t + 1)
                if last_use(t) is not None:
                    by_dve, count = evac_engine(last_use(t))
                    pe.wait_ge(evac_dve if by_dve else evac_act, count)

            def tile(s, bank, mh, ml, gained=None):
                return split_product(pO[bank][:, 0:T], [(whi[s][:, c, :], wlo[s][:, c, :], mh[:, c, :], ml[:, c, :]) for c in range(C)], gained)

            def token_tiles(s, bank):
                last = None
                for b in range(TB):
                    tok = slice(b * P, (b + 1) * P)
                    last = split_product(pO[bank][:, b * 2 * P:(b + 1) * 2 * P],
                                         [(xhi[:, c, tok], xlo[:, c, tok], whis[:, s:s + 2, c, :], wlos[:, s:s + 2, c, :]) for c in range(C)])
                return last

            def square_sum(c, sem, count):
                pe.wait_ge(sem, count)
                ins = pe.matmul(pM[0][:, 0:T], ones[:], gates[:, c, :], start=c == 0, stop=c == C - 1)
                if c == C - 1:
                    ins.then_inc(ssq_done, 1)

            def rotate(k):
                pe.wait_ge(evac_dve, k + 1)
                if k >= 2:
                    pe.wait_ge(roped, k - 1)
                pe.matmul(pM[k % 2][:, 0:T], K("rot"), qkT[:, k, :], start=True, stop=True).then_inc(rot_done, 1)

            def scores(n):
                if 1 <= n <= UNITS_A:
                    pe.wait_ge(exp_done, 2 * n)
                elif n > UNITS_A:
                    pe.wait_ge(scores_taken, n - UNITS_A)
                last = None
                u = n if n < UNITS_A else n - UNITS_A
                h, b = u % HA, u // HA
                q0, k0 = (0, HA) if n < UNITS_A else (8, 12)
                if n == 0:
                    pe.wait_ge(roped, 2 * HA)
                if n == UNITS_A:
                    pe.wait_ge(evac_act, evac_engine(T_GATE - 1)[1])
                for m in range(2):
                    rows = slice(m * DH, (m + 1) * DH)
                    last = pe.matmul(pS[m][:, 0:T], qkT[rows, q0 + h, b * P:(b + 1) * P], qkT[rows, k0 + h, :],
                                     start=True, stop=True)
                last.then_inc(scores_done, 1)

            def turn(n):
                if n >= 2:
                    pe.wait_ge(turned_taken, n - 1)
                last = None
                if n < UNITS_A:
                    pe.wait_ge(dif_ready, n + 1)
                    for kb in range(TB):
                        last = pe.transpose(pT[n % 2][:, kb * P:(kb + 1) * P], dif[:, n % 2, kb * P:(kb + 1) * P], ident)
                else:
                    pe.wait_ge(exp_done, 2 * (n + 1))
                    if n < UNITS_A + 2:
                        pe.wait_ge(y_full, 2)
                    for m in range(2):
                        for kb in range(TB):
                            last = pe.transpose(pT[n % 2][:, m * T + kb * P:m * T + (kb + 1) * P], prob[:, n % 2, m, kb * P:(kb + 1) * P], ident)
                last.then_inc(probs_turned, 1)

            def times_v(n):
                pe.wait_ge(turned_taken, n + 1)
                if n >= 2:
                    pe.wait_ge(pv_taken, n - 1)
                last = None
                if n == 0:
                    pe.wait_ge(evac_act, evac_engine(T_QB - 1)[1])
                if n < UNITS_A:
                    for kb in range(TB):
                        last = pe.matmul(pM[n % 2][:, 0:P], probT[:, n % 2, kb * P:(kb + 1) * P], vtok[:, kb, n % HA, :],
                                         start=kb == 0, stop=kb == TB - 1)
                else:
                    pair = (n - UNITS_A) % HA
                    for m in range(2):
                        for kb in range(TB):
                            last = pe.matmul(pM[n % 2][:, m * DH:(m + 1) * DH], probT[:, n % 2, m * T + kb * P:m * T + (kb + 1) * P],
                                             vtok[:, kb, HA + pair, m * DH:(m + 1) * DH], start=kb == 0, stop=kb == TB - 1)
                last.then_inc(pv_done, 1)

            def turn_y(j):
                half, b = j // 2, j % 2
                if half == 0:
                    pe.wait_ge(y_ready, 1)
                    pe.wait_ge(turned_taken, UNITS_A)
                else:
                    pe.wait_ge(pv_taken, UNITS_A + UNITS_B)
                    pe.wait_ge(turned_taken, UNITS_A + UNITS_B)
                src = oA if half == 0 else oB
                last = None
                for h in range(HA):
                    last = pe.transpose(pT[j % 2][:, h * P:(h + 1) * P], src[:, b, h, :], ident)
                last.then_inc(y_turned, 1)

            for k in range(T_PROJ):
                if token_pair(k):
                    if k % 2 == 0:
                        tile_wait(k)
                        if k == T_VA:
                            pe.wait_ge(norm_lo, C)
                    else:
                        pe.wait_ge(lo_ready, k + 1)
                        token_tiles(k % RING - 1, bank_of(k)).then_inc(tile_done, 2)
                else:
                    tile_wait(k)
                    if k < T_VA:
                        tile(k % RING, bank_of(k), yhi, ylo, 0 if k == 0 else None).then_inc(tile_done, 1)
                    else:
                        tile(k % RING, bank_of(k), xhi, xlo).then_inc(tile_done, 1)
                if k == 0:
                    pe.wait_ge(ones_ready, 1)
                    for c in range(C):
                        square_sum(c, squares if c < C // 2 else squares_dve, 1)
                    pe.wait_ge(const_landed, 16 * 3)
                if 1 <= k <= T_VA:
                    rotate(k - 1)
                for n in units_at(k, 0):
                    scores(n)
                for n in units_at(k, 2):
                    turn(n)
                for n in units_at(k, 3):
                    times_v(n)
                if k in (T_GATE, T_GATE + 1):
                    turn_y(k - T_GATE)
                if k in (T_PROJ - 3, T_PROJ - 2):
                    turn_y(k - T_PROJ + 5)
            pe.wait_ge(y_lo, 4)
            pe.wait_ge(y_hi, 4)
            for k in range(T_PROJ, T_OUT):
                tile_wait(k)
                s = k % RING
                for half in range(2):
                    last = split_product(pO[k % 2][:, half * T:(half + 1) * T],
                                         [(whi[s][:, c, :], wlo[s][:, c, :], yhi[:, c, :], ylo[:, c, :]) for c in range(half * HA, (half + 1) * HA)])
                last.then_inc(tile_done, 1)
            pe.wait_ge(m_hi, C)
            pe.wait_ge(m_lo, C)
            for k in range(T_OUT, T_QUERY):
                tile_wait(k)
                tile(k % RING, k % 2, mhi, mlo).then_inc(tile_done, 1)
                if k >= T_OUT + 2:
                    square_sum(k - T_OUT - 2, squares, 1 + k - T_OUT - 1)
            square_sum(C - 2, squares, 1 + C - 1)
            for k in range(T_QUERY, T_U):
                tile_wait(k)
                tile(k % RING, k % 2, yhi, ylo, C if k == T_QUERY else None).then_inc(tile_done, 1)
                j = k - T_QUERY
                if j == 0:
                    square_sum(C - 1, squares, 1 + C)
                if j < 4:
                    b, q = j // 2, j % 2
                    if j >= 2:
                        pe.wait_ge(h1_taken, j - 1)
                    for c in range(4):
                        last = pe.transpose(pT[j % 2][:, c * P:(c + 1) * P], xT[:, q * 4 + c, b * P:(b + 1) * P], ident)
                    last.then_inc(h1_turned, 1)
            pe.wait_ge(norm_lo, 2 * C)
            pe.wait_ge(keys_landed, 16)
            pe.wait_ge(evac_dve, evac_engine(T_U - 1)[1])
            n = 0
            for i in range(8):
                b, q4 = i // 4, i % 4
                if i >= 2:
                    pe.wait_ge(sbank_taken, i - 1)
                for h in range(4):
                    hp = q4 * 4 + h
                    last = pe.matmul(pS[i % 2][:, h * P:(h + 1) * P], qp[:, hp, b * P:(b + 1) * P], keysT[:, hp, :], start=True, stop=True)
                last.then_inc(key_scores, 1)
                tile_wait(T_U + i)
                tile((T_U + i) % RING, i % 2, xhi, xlo).then_inc(tile_done, 1)

            base = act_takings(T_U)

            def u_tiles(start, stop, with_g):
                with pe.Fori(start // RING, stop // RING) as g:
                    for s in range(RING):
                        i = g * RING + s
                        pe.wait_ge(lo_ready, i + (T_U + 1))
                        pe.wait_ge(evac_act, i + (base - 1))
                        tile(s, s % 2, xhi, xlo).then_inc(tile_done, 1)
                        if with_g:
                            pe.wait_ge(onehot_ready, i - G_FIRST + 1)
                            pe.wait_ge(sbank_taken, i - G_FIRST + 7)
                            for tok in range(GTOK):
                                last = pe.matmul(pS[s % 2][:, tok * P:(tok + 1) * P], onehot[s % 2][:, 1, tok, :], onehot[s % 2][:, 0, tok, :],
                                                 start=True, stop=True)
                            last.then_inc(g_done, 1)

            def turn_route(b):
                pe.wait_ge(routed, b + 1)
                for a in range(3):
                    last = pe.transpose(pM[b][:, a * P:(a + 1) * P], route[:, b, a].rearrange("p h k -> p (h k)"), ident)
                last.then_inc(route_turned, 1)

            u_tiles(8, G_FIRST, False)
            turn_route(0)
            turn_route(1)
            u_tiles(G_FIRST, G_END, True)
            u_tiles(G_END, NE_TILES, False)

            pe.wait_ge(route_taken, 2)
            pe.wait_ge(h1_taken, 4)

            def v_tile(i, s, first=False, final=False):
                pe.wait_ge(lo_ready, i + (T_V + 1))
                pe.wait_ge(vlo_ready, i + 1)
                pe.wait_ge(glo_ready, i + 1)
                vh = whi[s].rearrange("p c n -> p (c n)")
                vl = wlo[s].rearrange("p c n -> p (c n)")
                last = None
                for b in range(TB):
                    wh, wl = ghi[s % 2][:, b * P:(b + 1) * P], glo[s % 2][:, b * P:(b + 1) * P]
                    for n, (st, mv) in enumerate(((wh, vh), (wh, vl), (wl, vh))):
                        for q in range(2):
                            last = pe.matmul(acc[b][q][:], st, mv[:, q * 512:(q + 1) * 512], start=first and n == 0, stop=final and n == 2)
                    if final:
                        last.then_inc(acc_done, 1)
                if not final:
                    last.then_inc(tile_done, 1)

            for s in range(RING):
                v_tile(s, s, first=s == 0)
            with pe.Fori(1, NE_TILES // RING - 1) as g:
                for s in range(RING):
                    v_tile(g * RING + s, s)
            for s in range(RING):
                v_tile(NE_TILES - RING + s, s, final=s == RING - 1)


def constants():
    c = np.zeros((P, N_CONST), np.float32)

    def put(name, a):
        c[:, CONST[name][0]:CONST[name][1]] = a

    put("iota16", np.arange(16, dtype=np.float32)[None, :])
    rope = DH // 4
    half = rope // 2
    inv = (np.float32(500000.0) ** (-np.arange(0, rope, 2, dtype=np.float32) / np.float32(rope))).astype(np.float32)
    ang = (np.arange(T, dtype=np.float32)[:, None] * inv[None, :]).astype(np.float32)
    rot = np.zeros((P, P), np.float32)
    cos = np.ones((P, T), np.float32)
    sin = np.zeros((P, T), np.float32)
    for m in range(2):
        for d in range(rope):
            p = m * DH + d
            rot[m * DH + (d + half) % rope, p] = 1.0
            cos[p] = np.cos(ang[:, d % half])
            sin[p] = np.sin(ang[:, d % half]) * (-1.0 if d < half else 1.0)
    put("rot", rot)
    put("cos", cos)
    put("sin", sin)
    colq = np.arange(P) % GRID_W
    start = np.clip(colq - KC // 2, 0, GRID_W - KC)
    ck = np.arange(GRID_W)
    put("mask", np.where((ck[None, :] >= start[:, None]) & (ck[None, :] < start[:, None] + KC), 0.0, MASKED).astype(np.float32))
    return c


def kernel(x, w_in, w_proj_a, w_proj_b, w_out, norm_mix, norm_ffn, norm_final,
           lambda_q1, lambda_k1, lambda_q2, lambda_k2, diff_subln, na_rpb,
           peer_w_query, peer_sub_keys, peer_u, peer_v):
    import concourse.bacc as bacc
    from concourse.bass_utils import run_bass_kernel_spmd

    def tiles(w):
        w = np.asarray(w)
        return w.reshape(C, P, -1, P).transpose(2, 1, 0, 3)

    w_proj = np.concatenate([np.asarray(w_proj_a)[0], np.asarray(w_proj_b)[0]], axis=0)
    stream = np.concatenate([tiles(np.asarray(w_in)[0]), tiles(w_proj), tiles(np.asarray(w_out)[0]),
                             tiles(np.asarray(peer_w_query)[0]), tiles(np.asarray(peer_u)[0].T)], axis=0)
    vrows = np.asarray(peer_v)[0].reshape(NE_TILES, P, C, P)
    xT = np.asarray(x)[0].T.reshape(C, P, T).transpose(1, 0, 2)
    cols = np.concatenate([np.asarray(norm_mix)[0].reshape(C, P).T, np.asarray(norm_ffn)[0].reshape(C, P).T,
                           np.asarray(diff_subln)[0].reshape(P, 1)], axis=1)
    keys = np.asarray(peer_sub_keys)[0].reshape(HP, NK, P).transpose(2, 0, 1)
    tok = np.arange(T)
    dr = tok[None, :] // GRID_W - tok[:, None] // GRID_W + KR_MAX - 1
    dc = np.clip(tok[None, :] % GRID_W - tok[:, None] % GRID_W + KC - 1, 0, 2 * KC - 2)
    bias = np.asarray(na_rpb)[0][:, dr, dc].reshape(HB, TB, P, T).transpose(2, 1, 0, 3)
    lamv = np.concatenate([np.asarray(v) for v in (lambda_q1, lambda_k1, lambda_q2, lambda_k2)], axis=0).reshape(1, 2, 2 * DH)

    idio = np.stack([np.eye(P, dtype=np.float32), np.broadcast_to(np.arange(P, dtype=np.float32), (P, P))], axis=1)

    nc = bacc.Bacc("TRN2", target_bir_lowering=False, num_devices=1)
    arrays, aps = {}, {}
    for name, a in (("stream", stream), ("vrows", vrows), ("xTin", xT), ("consts", constants()), ("idio", idio), ("cols", cols),
                    ("keys", keys), ("bias", bias), ("lamv", lamv), ("gfin", np.asarray(norm_final).reshape(1, D))):
        a = np.ascontiguousarray(a)
        arrays[f"in_{name}"] = a
        aps[name] = nc.dram_tensor(f"in_{name}", a.shape, mybir.dt.from_np(a.dtype), kind="ExternalInput").ap()
    h1_dram = nc.dram_tensor("h1_scratch", (P, TB, D), F32).ap()
    a_dram = nc.dram_tensor("a_scratch", (NE_TILES, P, T), F32).ap()
    out = nc.dram_tensor("out_0", (P, TB, D), F32, kind="ExternalOutput").ap()
    build(nc, aps["stream"], aps["vrows"], {"xT": aps["xTin"], "cst": aps["consts"], "idio": aps["idio"]}, aps["cols"], aps["keys"], aps["bias"],
          aps["lamv"], aps["gfin"], h1_dram, a_dram, out)
    r = run_bass_kernel_spmd(nc, [arrays], core_ids=[0])
    y = np.asarray(r.results[0]["out_0"])
    return y.transpose(1, 0, 2).reshape(1, T, D)
```

```python
from contextlib import ExitStack

import numpy as np

import concourse.bass as bass
from concourse import mybir

F32 = mybir.dt.float32
F32R = mybir.dt.float32r
U32 = mybir.dt.uint32
ALU = mybir.AluOpType
ACT = mybir.ActivationFunctionType
AX_X = mybir.AxisListType.X

P = 128
T = 256
TB = T // P
D = 1024
C = D // P
DH = 64
HA = 4
HB = 8
GRID_W, KC, KR_MAX = 64, 16, 8
ROWS = T // GRID_W
PH, NK, TOPK = 8, 128, 16
HP = PH * 2
EPS = 1e-6
LAM_INIT = 0.8 - 0.6 * float(np.exp(-0.0))
SCALE = DH ** -0.5
SINK = -3.0e38
MASKED = -1.0e30

T_QA, T_KA, T_VA = 0, HA, 2 * HA
T_QB = 3 * HA
T_KB, T_VB = T_QB + 4, T_QB + 8
T_GATE = T_QB + 12
T_PROJ = T_GATE + 16
T_OUT = T_PROJ + C
T_QUERY = T_OUT + C
T_U = T_QUERY + HP
NE_TILES = NK
T_V = T_U + NE_TILES
T_END = T_V + NE_TILES
RAW = 4
RING = 4
STORE_LAG = 7
LEAD = 3

UNROLL = 8

UNITS_A, UNITS_B = 8, 8
SLOT_A, SLOT_B = T_QB, T_GATE
G_FIRST = 60
GTOK = 4
GSUB = 2
G_STEPS = T // GTOK
G_END = G_FIRST + G_STEPS

CONST = {}
_at = 0
for _name, _n in (("ident", P), ("rot", P), ("cos", T), ("sin", T), ("iota16", 16), ("mask", GRID_W)):
    CONST[_name] = (_at, _at + _n)
    _at += _n
N_CONST = _at


def unit_slot(n):
    return SLOT_A + n if n < UNITS_A else SLOT_B + n - UNITS_A


def units_at(slot, lag):
    return [n for n in range(UNITS_A + UNITS_B) if unit_slot(n) + lag == slot]


def token_pair(t):
    return T_VA <= t < T_QB or T_VB <= t < T_GATE


def bank_of(t):
    return (t // 2) % 2 if token_pair(t) else t % 2


def last_use(t):
    return max((x for x in range(t) if bank_of(x) == bank_of(t)), default=None)


def evac_engine(t):
    dve = lambda x: x < T_VA or T_PROJ <= x < T_U
    same = [x for x in range(t + 1) if dve(x) == dve(t)]
    return dve(t), len(same)


def act_takings(t):
    return sum(not evac_engine(x)[0] for x in range(t))


def build(nc, stream, vrows, const, cols, keys, bias, lamv, gfin, h1_dram, a_dram, out):
    with ExitStack() as top:
        def psum(name, shape):
            return top.enter_context(nc.psum_tensor(name, shape, F32))

        def sem(name):
            return top.enter_context(nc.semaphore(name))

        def sbs(stack, name, shape, dt=F32):
            return stack.enter_context(nc.sbuf_tensor(name, shape, dt))

        raw = [sbs(top, f"raw{s}", [P, C, P]) for s in range(RAW)]
        whis = sbs(top, "whis", [P, RING, C, P], F32R)
        wlos = sbs(top, "wlos", [P, RING, C, P], F32R)
        whi = [whis[:, s] for s in range(RING)]
        wlo = [wlos[:, s] for s in range(RING)]
        with ExitStack() as front:
            cst = sbs(front, "cst", [P, N_CONST])
            col = sbs(front, "col", [P, 2 * C + 1])
            xT = sbs(front, "xT", [P, C, T])
            rstd = sbs(front, "rstd", [P, T])
            ones = sbs(front, "ones", [P, P])
            mx = sbs(front, "mx", [P, 16, 2])
            nmx = sbs(front, "nmx", [P, 16, 2])
            zs = sbs(front, "zs", [P, 16, 2])
            rz = sbs(front, "rz", [P, 16, 2])
            lam = sbs(front, "lam", [P, 8])
            ssA = sbs(front, "ssA", [P, 2, TB * HA])
            with ExitStack() as mixer:
                qkT = sbs(mixer, "qkT", [P, 16, T])
                gates = sbs(mixer, "gates", [P, 16, T])
                vtok = sbs(mixer, "vtok", [P, TB, 8, P])
                biasm = sbs(mixer, "biasm", [P, TB, HB, T])
                prob = sbs(mixer, "prob", [P, 2, 2, T])
                dif = sbs(mixer, "dif", [P, 2, T])
                probT = sbs(mixer, "probT", [P, 2, 2 * T])
                rtmp = sbs(mixer, "rtmp", [P, 2, T])
                oA = sbs(mixer, "oA", [P, TB, HA, P])
                oB = sbs(mixer, "oB", [P, TB, HA, P])
                yf = sbs(mixer, "yf", [P, HA, P])
                mtmp = sbs(mixer, "mtmp", [P, 2, T])
                mfull = sbs(mixer, "mfull", [P, 2, T])
                mhi = sbs(mixer, "mhi", [P, C, T], F32R)
                mlo = sbs(mixer, "mlo", [P, C, T], F32R)
                yhi = sbs(mixer, "yhi", [P, C, T], F32R)
                ylo = sbs(mixer, "ylo", [P, C, T], F32R)
            with ExitStack() as router:
                qp = sbs(router, "qp", [P, HP, T])
                qpad = sbs(router, "qpad", [P, 16, T])
                keysT = sbs(router, "keysT", [P, HP, NK])
                sc = sbs(router, "sc", [P, TB, HP, NK])
                scm = sbs(router, "scm", [P, NK])
                top_v = sbs(router, "top_v", [P, TB, HP, TOPK])
                top_i = sbs(router, "top_i", [P, TB, HP, TOPK], U32)
                top_f = sbs(router, "top_f", [P, TB, HP, TOPK])
                cand = sbs(router, "cand", [P, PH, TOPK * TOPK])
                candm = sbs(router, "candm", [P, TOPK * TOPK])
                pick_v = sbs(router, "pick_v", [P, PH, TOPK])
                pick_p = sbs(router, "pick_p", [P, PH, TOPK], U32)
                pick_h = sbs(router, "pick_h", [P, 2, PH, TOPK], U32)
                pick_f = sbs(router, "pick_f", [P, 2, PH, TOPK])
                eq = sbs(router, "eq", [P, PH * TOPK, TOPK])
                route = sbs(router, "route", [P, TB, 3, PH, TOPK])
                gsum = sbs(router, "gsum", [P, 2, PH])
                h1tok = sbs(router, "h1tok", [P, TB, D])
        G = sbs(top, "G", [P, NK, T])
        fin = sbs(top, "fin", [P, 10])
        iota = sbs(top, "iota", [P, P])[:]
        with ExitStack() as uphase:
            xhi = sbs(uphase, "xhi", [P, C, T], F32R)
            xlo = sbs(uphase, "xlo", [P, C, T], F32R)
            routeT = sbs(uphase, "routeT", [P, 3, T])
            ghiT = sbs(uphase, "ghiT", [P, T], F32R)
            hot1 = [sbs(uphase, f"hot1_{s}", [P, GSUB, P], F32R) for s in range(2)]
            hot2 = [sbs(uphase, f"hot2_{s}", [P, GSUB, P]) for s in range(2)]
            ghot = [sbs(uphase, f"ghot{s}", [P, GSUB, 2, P], F32R) for s in range(2)]
            ast = [sbs(uphase, f"ast{s}", [P, T]) for s in range(2)]
        with ExitStack() as vphase:
            htok = sbs(vphase, "htok", [P, TB, D])
            gf = sbs(vphase, "gf", [P, D])
            fsq = sbs(vphase, "fsq", [P, D])
            glo = [sbs(vphase, f"glo{s}", [P, T], F32R) for s in range(2)]
            vpad = sbs(vphase, "vpad", [P, 2, T])
            aring = [sbs(vphase, f"aring{s}", [P, T]) for s in range(4)]
            wfull = [sbs(vphase, f"wfull{s}", [P, T]) for s in range(2)]
            ghi = [sbs(vphase, f"ghi{s}", [P, T], F32R) for s in range(2)]

        def K(name):
            a, b = CONST[name]
            return cst[:, a:b]

        ident = K("ident")

        pO = [psum("pO0", [P, 512]), psum("pO1", [P, 512])]
        pSS = psum("pSS", [P, 2, 512])
        pS = [pSS[:, 0, :], pSS[:, 1, :]]
        pTT = psum("pTT", [P, 2, 512])
        pT = [pTT[:, 0, :], pTT[:, 1, :]]
        pG = [pSS, pTT]
        pM = [psum("pM0", [P, 512]), psum("pM1", [P, 512])]
        acc = [pT, [pM[0][:], pM[1][:]]]

        raw_landed = [sem(f"raw_landed{s}") for s in range(RAW)]
        x_landed = [sem("x_landed0"), sem("x_landed1")]
        gains_landed = sem("gains_landed")
        const_landed = sem("const_landed")
        ones_ready = sem("ones_ready")
        squares_dve = sem("squares_dve")
        bias_landed = sem("bias_landed")
        keys_landed = sem("keys_landed")
        hi_ready = sem("hi_ready")
        lo_ready = sem("lo_ready")
        tile_done = sem("tile_done")
        evac_act = sem("evac_act")
        evac_dve = sem("evac_dve")
        dve_order = sem("dve_order")
        squares = sem("squares")
        ssq_done = sem("ssq_done")
        meansq = sem("meansq")
        root = sem("root")
        normed = sem("normed")
        norm_hi = sem("norm_hi")
        norm_lo = sem("norm_lo")
        lam_sums = sem("lam_sums")
        lam_exps = sem("lam_exps")
        gain_hi = sem("gain_hi")
        gain_lo = sem("gain_lo")
        rot_done = sem("rot_done")
        roped = sem("roped")
        bias_masked = sem("bias_masked")
        scores_done = sem("scores_done")
        scores_taken = sem("scores_taken")
        max_ready = sem("max_ready")
        exp_done = sem("exp_done")
        dif_ready = sem("dif_ready")
        probs_turned = sem("probs_turned")
        turned_taken = sem("turned_taken")
        pv_done = sem("pv_done")
        pv_taken = sem("pv_taken")
        ya_meansq = sem("ya_meansq")
        ya_root = sem("ya_root")
        y_ready = sem("y_ready")
        y_turned = sem("y_turned")
        y_full = sem("y_full")
        y_hi = sem("y_hi")
        y_lo = sem("y_lo")
        m_full = sem("m_full")
        m_hi = sem("m_hi")
        m_lo = sem("m_lo")
        h1_turned = sem("h1_turned")
        h1_taken = sem("h1_taken")
        h1_stored = sem("h1_stored")
        key_scores = sem("key_scores")
        sbank_taken = sem("sbank_taken")
        pick_max = sem("pick_max")
        pick_exp = sem("pick_exp")
        routed = sem("routed")
        route_turned = sem("route_turned")
        gbanks_free = sem("gbanks_free")
        hot1_ready = sem("hot1_ready")
        hot2_ready = sem("hot2_ready")
        ghot_hi = sem("ghot_hi")
        ghot_lo = sem("ghot_lo")
        g_done = sem("g_done")
        g_copied = sem("g_copied")
        a_stored = [sem(f"a_stored{s}") for s in range(2)]
        a_landed = [sem(f"a_landed{s}") for s in range(4)]
        final_landed = sem("final_landed")
        w_ready = sem("w_ready")
        ghi_ready = sem("ghi_ready")
        glo_ready = sem("glo_ready")
        vlo_ready = sem("vlo_ready")
        acc_done = sem("acc_done")
        h2_ready = sem("h2_ready")
        fin_sum = sem("fin_sum")
        fin_ms = sem("fin_ms")
        fin_root = sem("fin_root")
        out_ready = sem("out_ready")
        out_stored = sem("out_stored")

        block = top.enter_context(nc.Block())

        @block.sync
        def _(sp):
            half = C // 2
            sp.dma_start(raw[0][:], stream[0]).then_inc(raw_landed[0], 16)
            sp.dma_start(col[:], cols).then_inc(gains_landed, 16)
            for q in range(2):
                sp.dma_start(xT[:, q * half:(q + 1) * half, :], const["xT"][:, q * half:(q + 1) * half, :]).then_inc(x_landed[q], 16)
            sp.dma_start(raw[1][:], stream[1]).then_inc(raw_landed[1], 16)
            sp.dma_start(rtmp[:, :, 0:2 * DH], lamv.to_broadcast([P, 2, 2 * DH])).then_inc(const_landed, 16)
            sp.dma_start(cst[:], const["cst"]).then_inc(const_landed, 16)
            for t in range(2, RAW):
                sp.dma_start(raw[t][:], stream[t]).then_inc(raw_landed[t], 16)
            sp.dma_start(iota, const["count"]).then_inc(const_landed, 16)

            def load(t, s, row):
                sp.wait_ge(lo_ready, t - RAW + 1)
                sp.dma_start(raw[s][:], row).then_inc(raw_landed[s], 16)

            for t in range(RAW, 2 * RAW):
                load(t, t % RAW, stream[t])
            sp.dma_start(biasm[:], bias).then_inc(bias_landed, 16)
            with sp.Fori(2, T_QUERY // RAW + 1) as g:
                for s in range(RAW):
                    load(g * RAW + s, s, stream[bass.ds(g * RAW + s, 1)])
            sp.wait_ge(tile_done, T_OUT)
            sp.dma_start(keysT[:], keys).then_inc(keys_landed, 16)
            with sp.Fori(T_QUERY // RAW + 1, T_U // RAW) as g:
                for s in range(RAW):
                    load(g * RAW + s, s, stream[bass.ds(g * RAW + s, 1)])
            sp.wait_ge(h1_taken, 4)
            sp.dma_start(h1_dram, h1tok[:]).then_inc(h1_stored, 16)

            def store(i, s2):
                sp.wait_ge(evac_act, i + (act_takings(T_U) + 1))
                sp.dma_start(a_dram[i] if isinstance(i, int) else a_dram[bass.ds(i, 1)], ast[s2][:]).then_inc(a_stored[s2], 16)

            for t in range(T_U, T_U + 2 * RAW):
                load(t, t % RAW, stream[t])
                if t >= T_U + STORE_LAG:
                    store(t - T_U - STORE_LAG, (t - T_U - STORE_LAG) % 2)
            with sp.Fori(T_U // RAW + 2, T_V // RAW) as g:
                for s in range(RAW):
                    load(g * RAW + s, s, stream[bass.ds(g * RAW + s, 1)])
                    store(g * RAW + (s - T_U - STORE_LAG), (s + STORE_LAG) % 2)
            for s in range(RAW):
                load(T_V + s, s, vrows[s:s + 1])
                i = NE_TILES + s - STORE_LAG
                store(i, i % 2)
            lower, upper = slice(0, C // 2), slice(C // 2, C)

            def load_v(i, s):
                row = vrows[i] if isinstance(i, int) else vrows[bass.ds(i, 1)].rearrange("o p c n -> (o p) c n")
                sp.wait_ge(lo_ready, i + (T_V - RAW + 1))
                sp.dma_start(raw[s][:, lower, :], row[:, lower, :]).then_inc(raw_landed[s], 16)
                sp.wait_ge(vlo_ready, i - RAW + 1)
                sp.dma_start(raw[s][:, upper, :], row[:, upper, :]).then_inc(raw_landed[s], 16)

            def load_a(i, s):
                sp.wait_ge(w_ready, i - 3)
                sp.dma_start(aring[s][:], a_dram[bass.ds(i, 1)] if not isinstance(i, int) else a_dram[i]).then_inc(a_landed[s], 16)

            for s in range(RAW):
                load_v(RAW + s, s)
                i = NE_TILES + RAW + s - STORE_LAG
                if i < NE_TILES:
                    store(i, i % 2)
                sp.wait_ge(a_stored[s % 2], 16 * ((RAW + s) // 2 + 1))
                load_a(RAW + s, s)
            for s in range(2):
                sp.wait_ge(a_stored[s], 16 * (NE_TILES // 2))
            sp.wait_ge(tile_done, T_V)
            sp.wait_ge(h1_stored, 16)
            sp.dma_start(gf[:], gfin.to_broadcast([P, D])).then_inc(final_landed, 16)
            sp.dma_start(htok[:], h1_dram).then_inc(final_landed, 16)
            with sp.Fori(2, NE_TILES // RAW) as g:
                for s in range(RAW):
                    load_v(g * RAW + s, s)
                    load_a(g * RAW + s, s)
            for j in range(2 * TB):
                sp.wait_ge(out_ready, j + 1)
                half = (slice(None), j // 2, slice((j % 2) * 512, (j % 2 + 1) * 512))
                sp.dma_start(out[half], htok[half]).then_inc(out_stored, 16)
            sp.wait_ge(out_stored, 16 * 2 * TB)

        @block.gpsimd
        def _(pool):
            pool.memset(ones[:], 1.0).then_inc(ones_ready, 1)

            def low(t, s):
                pool.wait_ge(hi_ready, t + 1)
                pool.tensor_tensor(wlo[s], raw[s][:], whi[s].bitcast(F32), ALU.subtract).then_inc(lo_ready, 1)

            pool.wait_ge(lo_ready, 1)
            for t in range(1, T_QB):
                low(t, t % RING)
            with pool.Fori(T_QB // RING, T_V // RING) as g:
                for s in range(RING):
                    low(g * RING + s, s)
            with pool.Fori(T_V // RING, T_END // RING) as g:
                for s in range(RING):
                    pool.wait_ge(hi_ready, g * RING + s + 1)
                    pool.tensor_tensor(wlo[s][:, 0:C // 2, :], raw[s][:, 0:C // 2, :], whi[s][:, 0:C // 2, :].bitcast(F32),
                                       ALU.subtract).then_inc(lo_ready, 1)

        @block.scalar
        def _(act):
            def hi(t, s, turn):
                act.wait_ge(raw_landed[s], turn * 16)
                if not (isinstance(t, int) and t < RING):
                    act.wait_ge(tile_done, t - RING + 1)
                act.activation(whi[s], raw[s][:], ACT.Copy).then_inc(hi_ready, 1)

            def landings(t):
                return t // RAW + 1 + max(0, t // RAW - T_V // RAW)

            def hi_at(t):
                if t < T_END:
                    hi(t, t % RING, landings(t))

            def gained_hi(gain0, c):
                act.activation(yhi[:, c, :], xT[:, c, :], ACT.Copy, scale=col[:, gain0 + c:gain0 + c + 1]).then_inc(gain_hi, 1)

            def rms_root(k):
                act.wait_ge(meansq, k)
                act.activation(rstd[:], rstd[:], ACT.Sqrt).then_inc(root, 1)

            def normed_hi(k, c):
                act.wait_ge(normed, C * (k - 1) + c + 1)
                act.activation(xhi[:, c, :], gates[:, c, :], ACT.Copy).then_inc(norm_hi, 1)

            act.preload_act_table(ACT.Sqrt)
            hi_at(0)
            act.wait_ge(gains_landed, 16)
            for c in range(C):
                act.wait_ge(x_landed[c // (C // 2)], 16)
                gained_hi(0, c)
            hi_at(1)
            act.activation(gates[:, 0:C // 2, :], xT[:, 0:C // 2, :], ACT.Square).then_inc(squares, 1)
            hi_at(2)
            hi_at(3)
            rms_root(1)
            act.wait_ge(lam_sums, 1)
            act.activation(lam[:, 2:4], lam[:, 0:2], ACT.Exp).then_inc(lam_exps, 1)
            for k in range(T_PROJ):
                if k:
                    hi_at(k + LEAD)
                if 1 <= k <= C // 2:
                    normed_hi(1, 2 * k - 2)
                    normed_hi(1, 2 * k - 1)
                if token_pair(k):
                    if k % 2:
                        act.wait_ge(tile_done, k + 1)
                        v = k - 1 - T_VA if k < T_QB else k - 1 - T_VB + HA
                        act.activation(vtok[:, :, v:v + 2, :], pO[bank_of(k)][:].rearrange("p (b v n) -> p b v n", b=TB, v=2),
                                       ACT.Copy).then_inc(evac_act, 2)
                elif k >= T_VA:
                    act.wait_ge(tile_done, k + 1)
                    src = pO[bank_of(k)][:, 0:T]
                    if k >= T_GATE:
                        act.activation(gates[:, k - T_GATE, :], src, ACT.Tanh, scale=0.5).then_inc(evac_act, 1)
                    else:
                        act.activation(qkT[:, k - T_QB + 8, :], src, ACT.Copy).then_inc(evac_act, 1)
                for n in units_at(k, 0):
                    act.wait_ge(max_ready, n + 1)
                    if n >= 2:
                        if n - 2 < UNITS_A:
                            act.wait_ge(dif_ready, n - 1)
                        else:
                            act.wait_ge(probs_turned, n - 1)
                    for m in range(2):
                        src, scale = (pS[m][:, 0:T], SCALE) if n < UNITS_A else (prob[:, n % 2, m, :], 1.0)
                        act.activation(prob[:, n % 2, m, :], src, ACT.Exp, bias=nmx[:, n, m:m + 1], scale=scale,
                                       accum_out=zs[:, n, m:m + 1]).then_inc(exp_done, 1)
                if k == T_GATE - 1:
                    act.wait_ge(ya_meansq, 1)
                    act.activation(ssA[:, 0, :], ssA[:, 0, :], ACT.Sqrt).then_inc(ya_root, 1)
                for j in {T_GATE + 1: (0, 1), T_PROJ - 3: (2,), T_PROJ - 2: (3,)}.get(k, ()):
                    act.wait_ge(y_full, j + 1)
                    half, b = j // 2, j % 2
                    act.activation(yhi[:, half * HA:(half + 1) * HA, b * P:(b + 1) * P], yf[:], ACT.Copy).then_inc(y_hi, 1)
            for k in range(T_PROJ, T_QUERY):
                hi_at(k + LEAD)
                if k < T_OUT:
                    j = k - T_PROJ
                    act.wait_ge(m_full, j + 1)
                    act.activation(mhi[:, j, :], mfull[:, j % 2, :], ACT.Copy).then_inc(m_hi, 1)
                elif k == T_OUT:
                    act.preload_act_table(ACT.Sqrt)
                if k >= T_OUT:
                    act.wait_ge(evac_dve, evac_engine(k)[1])
                    gained_hi(C, k - T_OUT)
                    act.activation(gates[:, k - T_OUT, :], xT[:, k - T_OUT, :], ACT.Square).then_inc(squares, 1)
            for k in range(T_QUERY, T_U):
                hi_at(k + LEAD)
                if k == T_QUERY:
                    rms_root(2)
                if k - T_QUERY < C:
                    normed_hi(2, k - T_QUERY)
            act.preload_act_table(ACT.Gelu)

            def gelu(t, i, s2, turns):
                act.wait_ge(tile_done, t + 1)
                if turns is not None:
                    act.wait_ge(a_stored[s2], turns)
                act.activation(ast[s2][:], pO[s2][:, 0:T], ACT.Gelu).then_inc(evac_act, 1)

            for i in range(8):
                hi_at(T_U + i + LEAD)
                n = i
                act.wait_ge(key_scores, n + 1)
                b, q4 = n // 4, n % 4
                act.activation(sc[:, b, q4 * 4:(q4 + 1) * 4, :], pS[n % 2].rearrange("p (h k) -> p h k", h=4), ACT.Copy).then_inc(sbank_taken, 1)
                gelu(T_U + i, i, i % 2, None if i < 2 else 16 * (i // 2))

            def u_step(g, s):
                i = g * 4 + s
                hi(i + (T_U + LEAD), (s + LEAD) % RING, g + (T_U // RAW + (s + LEAD) // RAW + 1))
                gelu(i + T_U, i, s % 2, (g * 2 + s // 2) * 16)
                return i

            for b, (i0, stop) in enumerate(((8, 20), (20, 40))):
                with act.Fori(i0 // 4, stop // 4) as g:
                    for s in range(4):
                        u_step(g, s)
                act.wait_ge(pick_max, b + 1)
                act.activation(route[:, b, 2, :, :], route[:, b, 2, :, :], ACT.Exp).then_inc(pick_exp, 1)
                act.preload_act_table(ACT.Gelu)
            with act.Fori(40 // 4, G_FIRST // 4) as g:
                for s in range(4):
                    u_step(g, s)
            def low_hot(u, p):
                act.wait_ge(hot2_ready, u + 1)
                for tok in range(GSUB):
                    at = u * GSUB + tok
                    ins = act.activation(ghot[p][:, tok, 1, :], hot2[p][:, tok, :], ACT.Copy,
                                         scale=routeT[:, 2, at:at + 1] if isinstance(u, int) else routeT[:, 2, bass.ds(at, 1)])
                ins.then_inc(ghot_lo, 1)

            def g_step(g, s, more=True):
                i = g * 4 + s
                k = i - G_FIRST
                hi(i + (T_U + LEAD), (s + LEAD) % RING, g + (T_U // RAW + (s + LEAD) // RAW + 1))
                if more:
                    low_hot(k * 2 + 2, 0)
                gelu(i + T_U, i, s % 2, (g * 2 + s // 2) * 16)
                act.wait_ge(g_done, k * 2 + 2)
                act.activation(G[:, :, bass.ds(k * GTOK, GTOK)].rearrange("p i t -> p t i"),
                               pG[s % 2][:].rearrange("p b (t h i) -> p (b t) h i", t=GSUB, h=2)[:, :, 0], ACT.Copy).then_inc(g_copied, 1)
                if more:
                    low_hot(k * 2 + 3, 1)

            low_hot(0, 0)
            low_hot(1, 1)
            with act.Fori(G_FIRST // 4, G_END // 4 - 1) as g:
                for s in range(4):
                    g_step(g, s)
            for s in range(4):
                g_step(G_END // 4 - 1, s, more=s < 3)
            act.wait_ge(ghot_lo, 2 * G_STEPS)
            for s in range(4):
                act.wait_ge(a_stored[s % 2], 16 * (s // 2 + 1))
                act.dma_start(aring[s][:], a_dram[s]).then_inc(a_landed[s], 16)

            def w_hi(i, s):
                act.wait_ge(w_ready, i + 1)
                if not (isinstance(i, int) and i < 2):
                    act.wait_ge(tile_done, i + (T_V - 1))
                act.activation(ghi[s % 2][:], wfull[s % 2][:], ACT.Copy).then_inc(ghi_ready, 1)

            for s in range(4):
                u_step(G_END // 4, s)
                if s in (1, 2):
                    w_hi(s - 1, s - 1)
            with act.Fori(0, NE_TILES // 4 - 1) as g:
                for s in range(4):
                    hi(g * 4 + (s + T_V + LEAD), (s + LEAD) % RING, g * 2 + landings(T_V + s + LEAD))
                    w_hi(g * 4 + (s + 2), s + 2)
            for i in range(NE_TILES - 4, NE_TILES - 2):
                hi_at(T_V + i + LEAD)
                w_hi(i + 2, i + 2)
            act.preload_act_table(ACT.Sqrt)

            def half_sum(j):
                act.wait_ge(h2_ready, j + 1)
                if j >= 2:
                    act.wait_ge(fin_sum, j - 1)
                act.activation(fsq[:, (j % 2) * 512:(j % 2 + 1) * 512], htok[:, j // 2, (j % 2) * 512:(j % 2 + 1) * 512], ACT.Square,
                               accum_out=fin[:, j:j + 1]).then_inc(fin_sum, 1)

            def fin_rms(b):
                act.wait_ge(fin_ms, b + 1)
                act.activation(fin[:, 6 + b:7 + b], fin[:, 4 + b:5 + b], ACT.Sqrt, scale=1.0 / D).then_inc(fin_root, 1)

            half_sum(0)
            half_sum(1)
            half_sum(2)
            fin_rms(0)
            half_sum(3)
            fin_rms(1)

        @block.vector
        def _(dve):
            order = [0]

            def link(ins):
                order[0] += 1
                ins.then_inc(dve_order, 1)
                dve.wait_ge(dve_order, order[0])

            def gained_low(gain0, c):
                done = (C if gain0 else 0) + c + 1
                dve.wait_ge(gain_hi, done)
                dve.scalar_tensor_tensor(ylo[:, c, :], xT[:, c, :], col[:, gain0 + c:gain0 + c + 1], yhi[:, c, :].bitcast(F32),
                                         ALU.mult, ALU.subtract).then_inc(gain_lo, 1)

            def rms(k):
                dve.wait_ge(ssq_done, k)
                dve.tensor_scalar(rstd[:], pM[0][:, 0:T], 1.0 / D, EPS, ALU.mult, ALU.add).then_inc(meansq, 1)
                dve.wait_ge(root, k)
                link(dve.reciprocal(rstd[:], rstd[:]))

            def normed_full(k, gain0, c):
                dve.scalar_tensor_tensor(gates[:, c, :], xT[:, c, :], col[:, gain0 + c:gain0 + c + 1], rstd[:],
                                         ALU.mult, ALU.mult).then_inc(normed, 1)

            def normed_low(k, c):
                done = C * (k - 1) + c + 1
                dve.wait_ge(normed, done)
                dve.wait_ge(norm_hi, done)
                dve.tensor_tensor(xlo[:, c, :], gates[:, c, :], xhi[:, c, :].bitcast(F32), ALU.subtract).then_inc(norm_lo, 1)

            dve.wait_ge(hi_ready, 1)
            dve.tensor_tensor(wlo[0], raw[0][:], whi[0].bitcast(F32), ALU.subtract).then_inc(lo_ready, 1)
            dve.wait_ge(gains_landed, 16)
            for c in range(C):
                dve.wait_ge(x_landed[c // (C // 2)], 16)
                gained_low(0, c)
            dve.tensor_tensor(gates[:, C // 2:C, :], xT[:, C // 2:C, :], xT[:, C // 2:C, :], ALU.mult).then_inc(squares_dve, 1)
            dve.wait_ge(const_landed, 16 * 3)
            for m in range(2):
                link(dve.tensor_tensor(mtmp[:, m, 0:DH], rtmp[:, m, 0:DH], rtmp[:, m, DH:2 * DH], ALU.mult))
            dve.tensor_reduce(lam[:, 0:2], mtmp[:, :, 0:DH], AX_X, ALU.add).then_inc(lam_sums, 1)
            rms(1)

            def lambda_rest():
                dve.wait_ge(lam_exps, 1)
                link(dve.tensor_tensor(lam[:, 4:5], lam[:, 3:4], lam[:, 2:3], ALU.subtract))
                link(dve.tensor_scalar(lam[:, 5:6], lam[:, 4:5], -LAM_INIT, None, ALU.add))
                link(dve.tensor_scalar(lam[:, 6:7], col[:, 2 * C:2 * C + 1], 1.0 - LAM_INIT, None, ALU.mult))

            def take_turned(n):
                if n >= 2:
                    dve.wait_ge(pv_done, n - 1)
                dve.wait_ge(probs_turned, n + 1)
                w = T if n < UNITS_A else 2 * T
                dve.tensor_copy(probT[:, n % 2, 0:w], pT[n % 2][:, 0:w]).then_inc(turned_taken, 1)

            def take_pv(n):
                dve.wait_ge(pv_done, n + 1)
                if n < UNITS_A:
                    h, b = n % HA, n // HA
                    dve.tensor_copy(oA[:, b, h, :], pM[n % 2][:, 0:P]).then_inc(pv_taken, 1)
                else:
                    h, b = (n - UNITS_A) % HA, (n - UNITS_A) // HA
                    dve.tensor_tensor(oB[:, b, h, :].rearrange("p (m v) -> p m v", m=2),
                                      pM[n % 2][:, 0:P].rearrange("p (m v) -> p m v", m=2),
                                      rz[:, n, :].unsqueeze(2).to_broadcast([P, 2, DH]), ALU.mult).then_inc(pv_taken, 1)

            def y_parts(j):
                half, b = j // 2, j % 2
                dve.wait_ge(y_turned, j + 1)
                if j:
                    dve.wait_ge(y_lo, j)
                src = pT[j % 2].rearrange("p (h t) -> p h t", h=HA)
                if half == 0:
                    dve.tensor_scalar(yf[:], src, lam[:, 6:7], None, ALU.mult).then_inc(y_full, 1)
                else:
                    dve.tensor_copy(yf[:], src).then_inc(y_full, 1)
                dve.wait_ge(y_full, j + 1)
                dve.wait_ge(y_hi, j + 1)
                at = (slice(None), slice(half * HA, (half + 1) * HA), slice(b * P, (b + 1) * P))
                dve.tensor_tensor(ylo[at], yf[:], yhi[at].bitcast(F32), ALU.subtract).then_inc(y_lo, 1)

            bview = biasm[:].rearrange("p b h (r c) -> p b (h r) c", c=GRID_W)

            for k in range(T_PROJ + 1):
                if k < T_VA:
                    dve.wait_ge(tile_done, k + 1)
                    dve.tensor_tensor(qkT[:, k, :], pO[k % 2][:, 0:T], rstd[:], ALU.mult).then_inc(evac_dve, 1)
                    chunks = (2 * k, 2 * k + 1) if 2 * k < C else ()
                    for c in chunks:
                        normed_full(1, 0, c)
                    dve.wait_ge(evac_dve, k + 1)
                    link(dve.tensor_tensor(rtmp[:, 0, :], qkT[:, k, :], K("cos"), ALU.mult))
                    for c in chunks:
                        normed_low(1, c)
                    dve.wait_ge(rot_done, k + 1)
                    link(dve.tensor_tensor(rtmp[:, 1, :], pM[k % 2][:, 0:T], K("sin"), ALU.mult))
                    dve.tensor_tensor(qkT[:, k, :], rtmp[:, 0, :], rtmp[:, 1, :], ALU.add).then_inc(roped, 1)
                    dve.wait_ge(roped, k + 1)
                    if k == 0:
                        lambda_rest()
                for n in units_at(k, 1):
                    dve.wait_ge(exp_done, 2 * (n + 1))
                    if n < UNITS_A:
                        link(dve.reciprocal(rz[:, n, :], zs[:, n, :]))
                        link(dve.tensor_tensor(rz[:, n, 1:2], rz[:, n, 1:2], lam[:, 5:6], ALU.mult))
                        if n >= 2:
                            dve.wait_ge(probs_turned, n - 1)
                        link(dve.tensor_scalar(rtmp[:, 0, :], prob[:, n % 2, 1, :], rz[:, n, 1:2], None, ALU.mult))
                        dve.scalar_tensor_tensor(dif[:, n % 2, :], prob[:, n % 2, 0, :], rz[:, n, 0:1], rtmp[:, 0, :],
                                                 ALU.mult, ALU.add).then_inc(dif_ready, 1)
                        dve.wait_ge(dif_ready, n + 1)
                    else:
                        link(dve.reciprocal(rz[:, n, :], zs[:, n, :]))
                for n in units_at(k, 0):
                    dve.wait_ge(scores_done, n + 1)
                    if n < UNITS_A:
                        link(dve.tensor_reduce(mx[:, n, :], pSS[:, :, 0:T], AX_X, ALU.max))
                        dve.tensor_scalar(nmx[:, n, :], mx[:, n, :], -SCALE, None, ALU.mult).then_inc(max_ready, 1)
                    else:
                        h, b = (n - UNITS_A) % HA, (n - UNITS_A) // HA
                        if n == UNITS_A:
                            dve.wait_ge(bias_masked, TB * ROWS)
                        if n - 2 >= UNITS_A:
                            dve.wait_ge(probs_turned, n - 1)
                        dve.scalar_tensor_tensor(prob[:, n % 2, :, :], pSS[:, :, 0:T], SCALE,
                                                 biasm[:, b, 2 * h:2 * h + 2, :], ALU.mult, ALU.add).then_inc(scores_taken, 1)
                        dve.wait_ge(scores_taken, n - UNITS_A + 1)
                        link(dve.tensor_reduce(mx[:, n, :], prob[:, n % 2, :, :], AX_X, ALU.max))
                        dve.tensor_scalar(nmx[:, n, :], mx[:, n, :], -1.0, None, ALU.mult).then_inc(max_ready, 1)
                for n in units_at(k, 2):
                    take_turned(n)
                for n in units_at(k, 3):
                    take_pv(n)
                if T_VA <= k < T_VA + TB * ROWS:
                    part = k - T_VA
                    dve.wait_ge(bias_landed, 16)
                    view = bview[:, part // ROWS, (part % ROWS) * HB:(part % ROWS + 1) * HB, :]
                    dve.tensor_tensor(view, view, K("mask").unsqueeze(1).to_broadcast([P, HB, GRID_W]), ALU.add).then_inc(bias_masked, 1)
                if k == T_GATE - 1:
                    dve.wait_ge(pv_taken, UNITS_A)
                    flat = oA[:].rearrange("p b h v -> p (b h) v")
                    sq = gates[:, 0:4, :].rearrange("p a b -> p (a b)").rearrange("p (u v) -> p u v", v=P)
                    link(dve.tensor_tensor(sq, flat, flat, ALU.mult))
                    link(dve.tensor_reduce(ssA[:, 1, :], sq, AX_X, ALU.add))
                    dve.tensor_scalar(ssA[:, 0, :], ssA[:, 1, :], 1.0 / P, EPS, ALU.mult, ALU.add).then_inc(ya_meansq, 1)
                    dve.wait_ge(ya_root, 1)
                    link(dve.reciprocal(ssA[:, 1, :], ssA[:, 0, :]))
                    dve.tensor_tensor(flat, flat, ssA[:, 1, :].unsqueeze(2).to_broadcast([P, TB * HA, P]), ALU.mult).then_inc(y_ready, 1)
                if k == T_GATE + 1:
                    y_parts(0)
                    y_parts(1)
                if k in (T_PROJ - 3, T_PROJ - 2):
                    y_parts(k - T_PROJ + 5)
            for k in range(T_PROJ, T_OUT):
                j = k - T_PROJ
                dve.wait_ge(tile_done, k + 1)
                if j == 0:
                    dve.wait_ge(evac_act, evac_engine(T_PROJ - 1)[1])
                link(dve.scalar_tensor_tensor(mtmp[:, 0, :], gates[:, j, :], 1.0, pO[k % 2][:, 0:T], ALU.add, ALU.mult))
                dve.scalar_tensor_tensor(mtmp[:, 1, :], gates[:, C + j, :], 1.0, pO[k % 2][:, T:2 * T], ALU.add, ALU.mult).then_inc(evac_dve, 1)
                dve.wait_ge(evac_dve, evac_engine(k)[1])
                dve.tensor_tensor(mfull[:, j % 2, :], mtmp[:, 0, :], mtmp[:, 1, :], ALU.add).then_inc(m_full, 1)
                dve.wait_ge(m_full, j + 1)
                dve.wait_ge(m_hi, j + 1)
                dve.tensor_tensor(mlo[:, j, :], mfull[:, j % 2, :], mhi[:, j, :].bitcast(F32), ALU.subtract).then_inc(m_lo, 1)
                dve.wait_ge(m_lo, j + 1)
            for k in range(T_OUT, T_QUERY):
                j = k - T_OUT
                dve.wait_ge(tile_done, k + 1)
                dve.scalar_tensor_tensor(xT[:, j, :], pO[k % 2][:, 0:T], 0.5, xT[:, j, :], ALU.mult, ALU.add).then_inc(evac_dve, 1)
                dve.wait_ge(evac_dve, evac_engine(k)[1])
                gained_low(C, j)
            for k in range(T_QUERY, T_U):
                j = k - T_QUERY
                dve.wait_ge(tile_done, k + 1)
                if j == 0:
                    rms(2)
                dve.tensor_tensor(qp[:, j, :], pO[k % 2][:, 0:T], rstd[:], ALU.mult).then_inc(evac_dve, 1)
                if j < C:
                    normed_full(2, C, j)
                if 1 <= j <= 4:
                    dve.wait_ge(h1_turned, j)
                    b, q = (j - 1) // 2, (j - 1) % 2
                    dve.tensor_copy(h1tok[:, b, q * 512:(q + 1) * 512], pT[(j - 1) % 2]).then_inc(h1_taken, 1)
                if j < C:
                    normed_low(2, j)

            def top16(vals, idx, src, work):
                link(dve.max(vals[:, 0:8], src))
                dve.max_index(idx[:, 0:8], vals[:, 0:8], src)
                link(dve.match_replace(work, vals[:, 0:8], src, SINK))
                link(dve.max(vals[:, 8:16], work))
                link(dve.max_index(idx[:, 8:16], vals[:, 8:16], work))

            for b in range(TB):
                for h in range(HP):
                    if h % 4 == 0:
                        dve.wait_ge(sbank_taken, b * 4 + h // 4 + 1)
                    top16(top_v[:, b, h, :], top_i[:, b, h, :], sc[:, b, h, :], scm[:])
                link(dve.tensor_copy(top_f[:, b], top_i[:, b]))
                for h in range(PH):
                    ins = dve.tensor_tensor(cand[:, h, :].rearrange("p (x y) -> p x y", x=TOPK),
                                            top_v[:, b, 2 * h, :].unsqueeze(2).to_broadcast([P, TOPK, TOPK]),
                                            top_v[:, b, 2 * h + 1, :].unsqueeze(1).to_broadcast([P, TOPK, TOPK]), ALU.add)
                    link(ins)
                for h in range(PH):
                    top16(pick_v[:, h, :], pick_p[:, h, :], cand[:, h, :], candm[:])
                dve.tensor_tensor(route[:, b, 2], pick_v[:], pick_v[:, :, 0:1].to_broadcast([P, PH, TOPK]), ALU.subtract).then_inc(pick_max, 1)
                link(dve.tensor_scalar(pick_h[:, 0], pick_p[:], 4, None, ALU.logical_shift_right))
                link(dve.tensor_scalar(pick_h[:, 1], pick_p[:], TOPK - 1, None, ALU.bitwise_and))
                link(dve.tensor_copy(pick_f[:], pick_h[:]))
                for q in range(2):
                    link(dve.tensor_tensor(eq[:], pick_f[:, q].rearrange("p h k -> p (h k)").unsqueeze(2).to_broadcast([P, PH * TOPK, TOPK]),
                                           K("iota16").unsqueeze(1).to_broadcast([P, PH * TOPK, TOPK]), ALU.is_equal))
                    for h in range(PH):
                        e3 = eq[:, h * TOPK:(h + 1) * TOPK, :]
                        ins = dve.tensor_tensor(e3, e3, top_f[:, b, 2 * h + q, :].unsqueeze(1).to_broadcast([P, TOPK, TOPK]), ALU.mult)
                        link(ins)
                    link(dve.tensor_reduce(route[:, b, q].rearrange("p h k -> p (h k)"), eq[:], AX_X, ALU.add))
                dve.wait_ge(pick_exp, b + 1)
                link(dve.tensor_reduce(gsum[:, 0, :], route[:, b, 2], AX_X, ALU.add))
                link(dve.reciprocal(gsum[:, 1, :], gsum[:, 0, :]))
                dve.tensor_tensor(route[:, b, 2], route[:, b, 2], gsum[:, 1, :].unsqueeze(2).to_broadcast([P, PH, TOPK]), ALU.mult).then_inc(routed, 1)
            for b in range(TB):
                dve.wait_ge(route_turned, b + 1)
                link(dve.tensor_copy(routeT[:, :, b * P:(b + 1) * P], pM[b][:, 0:3 * P].rearrange("p (a t) -> p a t", a=3)))
            dve.tensor_copy(ghiT[:], routeT[:, 2, :]).then_inc(gbanks_free, 1)
            dve.wait_ge(gbanks_free, 1)
            dve.tensor_tensor(routeT[:, 2, :], routeT[:, 2, :], ghiT[:].bitcast(F32), ALU.subtract).then_inc(gbanks_free, 1)
            dve.wait_ge(gbanks_free, 2)

            def one_hots(u, p):
                def row(src):
                    return src[:, bass.ds(u * GSUB, GSUB)].unsqueeze(2).to_broadcast([P, GSUB, P])
                io = iota.unsqueeze(1).to_broadcast([P, GSUB, P])
                if not (isinstance(u, int) and u < 2):
                    dve.wait_ge(g_done, u - 1)
                dve.tensor_tensor(hot2[p][:], row(routeT[:, 0]), io, ALU.is_equal).then_inc(hot2_ready, 1)
                dve.tensor_tensor(hot1[p][:], row(routeT[:, 1]), io, ALU.is_equal).then_inc(hot1_ready, 1)
                dve.wait_ge(hot2_ready, u + 1)
                dve.tensor_tensor(ghot[p][:, :, 0, :], hot2[p][:], row(ghiT[:].bitcast(F32)), ALU.mult).then_inc(ghot_hi, 1)

            def add_low(k, pair):
                dve.wait_ge(g_copied, k + 1)
                at = G[:, :, bass.ds(k * GTOK, GTOK)].rearrange("p i t -> p t i")
                dve.tensor_tensor(at, pG[pair][:].rearrange("p b (t h i) -> p (b t) h i", t=GSUB, h=2)[:, :, 1], at, ALU.add).then_inc(gbanks_free, 1)

            for u in range(4):
                one_hots(u, u % 2)
            with dve.Fori(0, G_STEPS // 2 - 1) as g:
                for q in range(2):
                    k = g * 2 + (q + 1)
                    one_hots(k * 2 + 2, 0)
                    add_low(g * 2 + q, q)
                    one_hots(k * 2 + 3, 1)
            add_low(G_STEPS - 2, 0)
            add_low(G_STEPS - 1, 1)

            dve.wait_ge(gbanks_free, 2 + G_STEPS)
            dve.wait_ge(g_done, 2 * G_STEPS)

            def weights(i, s, turn):
                dve.wait_ge(a_landed[s], turn * 16)
                dve.tensor_tensor(wfull[s % 2][:], aring[s][:], G[:, i, :] if isinstance(i, int) else G[:, bass.ds(i, 1), :], ALU.mult).then_inc(w_ready, 1)

            def low(i, s):
                dve.wait_ge(w_ready, i + 1)
                dve.wait_ge(ghi_ready, i + 1)
                dve.tensor_tensor(glo[s % 2][:], wfull[s % 2][:], ghi[s % 2][:].bitcast(F32), ALU.subtract).then_inc(glo_ready, 1)

            def v_low(i, s):
                dve.wait_ge(hi_ready, i + (T_V + 1))
                dve.tensor_tensor(wlo[s][:, C // 2:C, :], raw[s][:, C // 2:C, :], whi[s][:, C // 2:C, :].bitcast(F32),
                                  ALU.subtract).then_inc(vlo_ready, 1)

            def next_parts(i, s, turn):
                dve.wait_ge(glo_ready, i + 1)
                if not isinstance(i, int) or i + 2 < NE_TILES:
                    weights(i + 2, (s + 2) % 4, turn)
                low(i + 1, s + 1)
                if not isinstance(i, int) or i + LEAD < NE_TILES:
                    v_low(i + LEAD, (s + LEAD) % RING)

            weights(0, 0, 1)
            weights(1, 1, 1)
            low(0, 0)
            for i in range(LEAD):
                v_low(i, i)
            with dve.Fori(0, NE_TILES // 4 - 1) as g:
                for s in range(4):
                    next_parts(g * 4 + s, s, g + ((s + 2) // 4 + 1))
            for i in range(NE_TILES - 4, NE_TILES - 1):
                next_parts(i, i % 4, (i + 2) // 4 + 1)

            dve.wait_ge(final_landed, 32)
            def residual(j):
                b, q = j // 2, j % 2
                dve.wait_ge(acc_done, j + 1)
                part = htok[:, b, q * 512:(q + 1) * 512]
                dve.tensor_tensor(part, acc[b][q], part, ALU.add).then_inc(h2_ready, 1)

            def whole_sum(b):
                dve.wait_ge(fin_sum, 2 * b + 2)
                dve.scalar_tensor_tensor(fin[:, 4 + b:5 + b], fin[:, 2 * b:2 * b + 1], D * EPS, fin[:, 2 * b + 1:2 * b + 2],
                                         ALU.add, ALU.add).then_inc(fin_ms, 1)

            def inverse(b):
                dve.wait_ge(fin_root, b + 1)
                link(dve.reciprocal(fin[:, 8 + b:9 + b], fin[:, 6 + b:7 + b]))

            def rows_out(j):
                b, q = j // 2, j % 2
                dve.wait_ge(h2_ready, j + 1)
                part = htok[:, b, q * 512:(q + 1) * 512]
                dve.scalar_tensor_tensor(part, part, fin[:, 8 + b:9 + b], gf[:, q * 512:(q + 1) * 512], ALU.mult, ALU.mult).then_inc(out_ready, 1)

            residual(0)
            residual(1)
            residual(2)
            whole_sum(0)
            residual(3)
            inverse(0)
            rows_out(0)
            whole_sum(1)
            rows_out(1)
            inverse(1)
            rows_out(2)
            rows_out(3)

        @block.tensor
        def _(pe):
            def split_product(dst, terms, arriving=None):
                last = None
                for c, (sh, sl, mh, ml) in enumerate(terms):
                    if arriving is not None:
                        pe.wait_ge(arriving[0], arriving[1] + c + 1)
                    for q, (st, mv) in enumerate(((sh, mh), (sh, ml), (sl, mh))):
                        last = pe.matmul(dst, st, mv, start=(c == 0 and q == 0), stop=(c == len(terms) - 1 and q == 2))
                return last

            def tile_wait(t):
                pe.wait_ge(lo_ready, t + 1)
                if last_use(t) is not None:
                    by_dve, count = evac_engine(last_use(t))
                    pe.wait_ge(evac_dve if by_dve else evac_act, count)

            def tile(s, bank, mh, ml, arriving=None):
                return split_product(pO[bank][:, 0:T], [(whi[s][:, c, :], wlo[s][:, c, :], mh[:, c, :], ml[:, c, :]) for c in range(C)], arriving)

            def token_tiles(s, bank):
                last = None
                for b in range(TB):
                    tok = slice(b * P, (b + 1) * P)
                    last = split_product(pO[bank][:, b * 2 * P:(b + 1) * 2 * P],
                                         [(xhi[:, c, tok], xlo[:, c, tok], whis[:, s:s + 2, c, :], wlos[:, s:s + 2, c, :]) for c in range(C)])
                return last

            def square_sum(c, sem, count):
                pe.wait_ge(sem, count)
                ins = pe.matmul(pM[0][:, 0:T], ones[:], gates[:, c, :], start=c == 0, stop=c == C - 1)
                if c == C - 1:
                    ins.then_inc(ssq_done, 1)

            def rotate(k):
                pe.wait_ge(evac_dve, k + 1)
                if k >= 2:
                    pe.wait_ge(roped, k - 1)
                pe.matmul(pM[k % 2][:, 0:T], K("rot"), qkT[:, k, :], start=True, stop=True).then_inc(rot_done, 1)

            def scores(n):
                if 1 <= n <= UNITS_A:
                    pe.wait_ge(exp_done, 2 * n)
                elif n > UNITS_A:
                    pe.wait_ge(scores_taken, n - UNITS_A)
                last = None
                u = n if n < UNITS_A else n - UNITS_A
                h, b = u % HA, u // HA
                q0, k0 = (0, HA) if n < UNITS_A else (8, 12)
                if n == 0:
                    pe.wait_ge(roped, 2 * HA)
                if n == UNITS_A:
                    pe.wait_ge(evac_act, evac_engine(T_GATE - 1)[1])
                for m in range(2):
                    rows = slice(m * DH, (m + 1) * DH)
                    last = pe.matmul(pS[m][:, 0:T], qkT[rows, q0 + h, b * P:(b + 1) * P], qkT[rows, k0 + h, :],
                                     start=True, stop=True)
                last.then_inc(scores_done, 1)

            def turn(n):
                if n >= 2:
                    pe.wait_ge(turned_taken, n - 1)
                last = None
                if n < UNITS_A:
                    pe.wait_ge(dif_ready, n + 1)
                    for kb in range(TB):
                        last = pe.transpose(pT[n % 2][:, kb * P:(kb + 1) * P], dif[:, n % 2, kb * P:(kb + 1) * P], ident)
                else:
                    pe.wait_ge(exp_done, 2 * (n + 1))
                    if n < UNITS_A + 2:
                        pe.wait_ge(y_full, 2)
                    for m in range(2):
                        for kb in range(TB):
                            last = pe.transpose(pT[n % 2][:, m * T + kb * P:m * T + (kb + 1) * P], prob[:, n % 2, m, kb * P:(kb + 1) * P], ident)
                last.then_inc(probs_turned, 1)

            def times_v(n):
                pe.wait_ge(turned_taken, n + 1)
                if n >= 2:
                    pe.wait_ge(pv_taken, n - 1)
                last = None
                if n == 0:
                    pe.wait_ge(evac_act, evac_engine(T_QB - 1)[1])
                if n < UNITS_A:
                    for kb in range(TB):
                        last = pe.matmul(pM[n % 2][:, 0:P], probT[:, n % 2, kb * P:(kb + 1) * P], vtok[:, kb, n % HA, :],
                                         start=kb == 0, stop=kb == TB - 1)
                else:
                    pair = (n - UNITS_A) % HA
                    for m in range(2):
                        for kb in range(TB):
                            last = pe.matmul(pM[n % 2][:, m * DH:(m + 1) * DH], probT[:, n % 2, m * T + kb * P:m * T + (kb + 1) * P],
                                             vtok[:, kb, HA + pair, m * DH:(m + 1) * DH], start=kb == 0, stop=kb == TB - 1)
                last.then_inc(pv_done, 1)

            def turn_y(j):
                half, b = j // 2, j % 2
                if half == 0:
                    pe.wait_ge(y_ready, 1)
                    pe.wait_ge(turned_taken, UNITS_A)
                else:
                    pe.wait_ge(pv_taken, UNITS_A + UNITS_B)
                    pe.wait_ge(turned_taken, UNITS_A + UNITS_B)
                src = oA if half == 0 else oB
                last = None
                for h in range(HA):
                    last = pe.transpose(pT[j % 2][:, h * P:(h + 1) * P], src[:, b, h, :], ident)
                last.then_inc(y_turned, 1)

            for k in range(T_PROJ):
                if token_pair(k):
                    if k % 2 == 0:
                        tile_wait(k)
                        if k == T_VA:
                            pe.wait_ge(norm_lo, C)
                    else:
                        pe.wait_ge(lo_ready, k + 1)
                        token_tiles(k % RING - 1, bank_of(k)).then_inc(tile_done, 2)
                else:
                    tile_wait(k)
                    if k < T_VA:
                        tile(k % RING, bank_of(k), yhi, ylo, (gain_lo, 0) if k == 0 else None).then_inc(tile_done, 1)
                    else:
                        tile(k % RING, bank_of(k), xhi, xlo).then_inc(tile_done, 1)
                if k == 0:
                    pe.wait_ge(ones_ready, 1)
                    for c in range(C):
                        square_sum(c, squares if c < C // 2 else squares_dve, 1)
                    pe.wait_ge(const_landed, 16 * 3)
                if 1 <= k < T_VA or k == T_VA + 1:
                    rotate(min(k, T_VA) - 1)
                for n in units_at(k, 0):
                    scores(n)
                for n in units_at(k, 2):
                    turn(n)
                for n in units_at(k, 3):
                    times_v(n)
                if k == T_GATE + 1:
                    turn_y(0)
                    turn_y(1)
                if k in (T_PROJ - 3, T_PROJ - 2):
                    turn_y(k - T_PROJ + 5)
            pe.wait_ge(y_lo, 4)
            pe.wait_ge(y_hi, 4)
            for k in range(T_PROJ, T_OUT):
                tile_wait(k)
                s = k % RING
                for half in range(2):
                    last = split_product(pO[k % 2][:, half * T:(half + 1) * T],
                                         [(whi[s][:, c, :], wlo[s][:, c, :], yhi[:, c, :], ylo[:, c, :]) for c in range(half * HA, (half + 1) * HA)])
                last.then_inc(tile_done, 1)
            for k in range(T_OUT, T_QUERY):
                tile_wait(k)
                tile(k % RING, k % 2, mhi, mlo, (m_lo, 0) if k == T_OUT else None).then_inc(tile_done, 1)
                if k >= T_OUT + 2:
                    square_sum(k - T_OUT - 2, squares, 1 + k - T_OUT - 1)
            square_sum(C - 2, squares, 1 + C - 1)
            for k in range(T_QUERY, T_U):
                tile_wait(k)
                tile(k % RING, k % 2, yhi, ylo, (gain_lo, C) if k == T_QUERY else None).then_inc(tile_done, 1)
                j = k - T_QUERY
                if j == 0:
                    square_sum(C - 1, squares, 1 + C)
                if j < 4:
                    b, q = j // 2, j % 2
                    if j >= 2:
                        pe.wait_ge(h1_taken, j - 1)
                    for c in range(4):
                        last = pe.transpose(pT[j % 2][:, c * P:(c + 1) * P], xT[:, q * 4 + c, b * P:(b + 1) * P], ident)
                    last.then_inc(h1_turned, 1)
            pe.wait_ge(norm_lo, 2 * C)
            pe.wait_ge(keys_landed, 16)
            pe.wait_ge(evac_dve, evac_engine(T_U - 1)[1])
            for i in range(8):
                b, q4 = i // 4, i % 4
                if i >= 2:
                    pe.wait_ge(sbank_taken, i - 1)
                for h in range(4):
                    hp = q4 * 4 + h
                    last = pe.matmul(pS[i % 2][:, h * P:(h + 1) * P], qp[:, hp, b * P:(b + 1) * P], keysT[:, hp, :], start=True, stop=True)
                last.then_inc(key_scores, 1)
                tile_wait(T_U + i)
                tile((T_U + i) % RING, i % 2, xhi, xlo).then_inc(tile_done, 1)

            base = act_takings(T_U)

            def g_tokens(k, p, pair):
                u = k * 2 + (p + 1)
                pe.wait_ge(hot1_ready, u)
                pe.wait_ge(ghot_hi, u)
                pe.wait_ge(ghot_lo, u)
                for tok in range(GSUB):
                    last = pe.matmul(pG[pair][:, p, tok * 2 * P:(tok + 1) * 2 * P], hot1[p][:, tok, :],
                                     ghot[p][:, tok].rearrange("p h i -> p (h i)"), start=True, stop=True)
                last.then_inc(g_done, 1)

            def u_tiles(start, stop, with_g):
                with pe.Fori(0, (stop - start) // UNROLL) as g:
                    for n in range(UNROLL):
                        i = g * UNROLL + (n + start)
                        s = (n + start) % RING
                        pe.wait_ge(lo_ready, i + (T_U + 1))
                        pe.wait_ge(evac_act, i + (base - 1))
                        if not with_g:
                            tile(s, s % 2, xhi, xlo).then_inc(tile_done, 1)
                            continue
                        for half in range(2):
                            for c in range(half * C // 2, (half + 1) * C // 2):
                                for q, (st, mv) in enumerate(((whi, xhi), (whi, xlo), (wlo, xhi))):
                                    last = pe.matmul(pO[s % 2][:, 0:T], st[s][:, c, :], mv[:, c, :], start=c == 0 and q == 0, stop=c == C - 1 and q == 2)
                            if half:
                                last.then_inc(tile_done, 1)
                            else:
                                pe.wait_ge(gbanks_free, i - G_FIRST + 1)
                            g_tokens(i - G_FIRST, half, s % 2)

            def turn_route(b):
                pe.wait_ge(routed, b + 1)
                for a in range(3):
                    last = pe.transpose(pM[b][:, a * P:(a + 1) * P], route[:, b, a].rearrange("p h k -> p (h k)"), ident)
                last.then_inc(route_turned, 1)

            for i in range(8, G_FIRST % UNROLL + 8):
                tile_wait(T_U + i)
                tile(i % RING, i % 2, xhi, xlo).then_inc(tile_done, 1)
            u_tiles(G_FIRST % UNROLL + 8, G_FIRST - UNROLL, False)
            for i in range(G_FIRST - UNROLL, G_FIRST):
                if i == G_FIRST - 2:
                    turn_route(0)
                    turn_route(1)
                tile_wait(T_U + i)
                tile(i % RING, i % 2, xhi, xlo).then_inc(tile_done, 1)
            u_tiles(G_FIRST, G_END, True)
            for i in range(G_END, NE_TILES):
                tile_wait(T_U + i)
                tile(i % RING, i % 2, xhi, xlo).then_inc(tile_done, 1)

            pe.wait_ge(gbanks_free, 2 + G_STEPS)

            def v_tile(i, s, first=False, final=False):
                pe.wait_ge(lo_ready, i + (T_V + 1))
                pe.wait_ge(vlo_ready, i + 1)
                pe.wait_ge(glo_ready, i + 1)
                vh = whi[s].rearrange("p c n -> p (c n)")
                vl = wlo[s].rearrange("p c n -> p (c n)")
                last = None
                for b in range(TB):
                    wh, wl = ghi[s % 2][:, b * P:(b + 1) * P], glo[s % 2][:, b * P:(b + 1) * P]
                    terms = list(enumerate(((wh, vh), (wh, vl), (wl, vh))))
                    steps = [(n, t, q) for q in range(2) for n, t in terms] if final else [(n, t, q) for n, t in terms for q in range(2)]
                    for n, (st, mv), q in steps:
                        last = pe.matmul(acc[b][q], st, mv[:, q * 512:(q + 1) * 512], start=first and n == 0, stop=final and n == 2)
                        if final and n == 2:
                            last.then_inc(acc_done, 1)
                if not final:
                    last.then_inc(tile_done, 1)

            for s in range(RING):
                v_tile(s, s, first=s == 0)
            with pe.Fori(0, (NE_TILES - 2 * RING) // UNROLL) as g:
                for n in range(UNROLL):
                    v_tile(g * UNROLL + (n + RING), n % RING)
            for s in range(RING):
                v_tile(NE_TILES - RING + s, s, final=s == RING - 1)


def constants():
    c = np.zeros((P, N_CONST), np.float32)

    def put(name, a):
        c[:, CONST[name][0]:CONST[name][1]] = a

    put("ident", np.eye(P, dtype=np.float32))
    put("iota16", np.arange(16, dtype=np.float32)[None, :])
    rope = DH // 4
    half = rope // 2
    inv = (np.float32(500000.0) ** (-np.arange(0, rope, 2, dtype=np.float32) / np.float32(rope))).astype(np.float32)
    ang = (np.arange(T, dtype=np.float32)[:, None] * inv[None, :]).astype(np.float32)
    rot = np.zeros((P, P), np.float32)
    cos = np.ones((P, T), np.float32)
    sin = np.zeros((P, T), np.float32)
    for m in range(2):
        for d in range(rope):
            p = m * DH + d
            rot[m * DH + (d + half) % rope, p] = 1.0
            cos[p] = np.cos(ang[:, d % half])
            sin[p] = np.sin(ang[:, d % half]) * (-1.0 if d < half else 1.0)
    put("rot", rot)
    put("cos", cos)
    put("sin", sin)
    colq = np.arange(P) % GRID_W
    start = np.clip(colq - KC // 2, 0, GRID_W - KC)
    ck = np.arange(GRID_W)
    put("mask", np.where((ck[None, :] >= start[:, None]) & (ck[None, :] < start[:, None] + KC), 0.0, MASKED).astype(np.float32))
    return c


def kernel(x, w_in, w_proj_a, w_proj_b, w_out, norm_mix, norm_ffn, norm_final,
           lambda_q1, lambda_k1, lambda_q2, lambda_k2, diff_subln, na_rpb,
           peer_w_query, peer_sub_keys, peer_u, peer_v):
    import concourse.bacc as bacc
    from concourse.bass_utils import run_bass_kernel_spmd

    def tiles(w):
        w = np.asarray(w)
        return w.reshape(C, P, -1, P).transpose(2, 1, 0, 3)

    w_proj = np.concatenate([np.asarray(w_proj_a)[0], np.asarray(w_proj_b)[0]], axis=0)
    stream = np.concatenate([tiles(np.asarray(w_in)[0]), tiles(w_proj), tiles(np.asarray(w_out)[0]),
                             tiles(np.asarray(peer_w_query)[0]), tiles(np.asarray(peer_u)[0].T)], axis=0)
    vrows = np.asarray(peer_v)[0].reshape(NE_TILES, P, C, P)
    xT = np.asarray(x)[0].T.reshape(C, P, T).transpose(1, 0, 2)
    cols = np.concatenate([np.asarray(norm_mix)[0].reshape(C, P).T, np.asarray(norm_ffn)[0].reshape(C, P).T,
                           np.asarray(diff_subln)[0].reshape(P, 1)], axis=1)
    keys = np.asarray(peer_sub_keys)[0].reshape(HP, NK, P).transpose(2, 0, 1)
    tok = np.arange(T)
    dr = tok[None, :] // GRID_W - tok[:, None] // GRID_W + KR_MAX - 1
    dc = np.clip(tok[None, :] % GRID_W - tok[:, None] % GRID_W + KC - 1, 0, 2 * KC - 2)
    bias = np.asarray(na_rpb)[0][:, dr, dc].reshape(HB, TB, P, T).transpose(2, 1, 0, 3)
    lamv = np.concatenate([np.asarray(v) for v in (lambda_q1, lambda_k1, lambda_q2, lambda_k2)], axis=0).reshape(1, 2, 2 * DH)

    count = np.broadcast_to(np.arange(P, dtype=np.float32), (P, P))

    nc = bacc.Bacc("TRN2", target_bir_lowering=False, num_devices=1)
    arrays, aps = {}, {}
    for name, a in (("stream", stream), ("vrows", vrows), ("xTin", xT), ("consts", constants()), ("count", count), ("cols", cols),
                    ("keys", keys), ("bias", bias), ("lamv", lamv), ("gfin", np.asarray(norm_final).reshape(1, D))):
        a = np.ascontiguousarray(a)
        arrays[f"in_{name}"] = a
        aps[name] = nc.dram_tensor(f"in_{name}", a.shape, mybir.dt.from_np(a.dtype), kind="ExternalInput").ap()
    h1_dram = nc.dram_tensor("h1_scratch", (P, TB, D), F32).ap()
    a_dram = nc.dram_tensor("a_scratch", (NE_TILES, P, T), F32).ap()
    out = nc.dram_tensor("out_0", (P, TB, D), F32, kind="ExternalOutput").ap()
    build(nc, aps["stream"], aps["vrows"], {"xT": aps["xTin"], "cst": aps["consts"], "count": aps["count"]}, aps["cols"], aps["keys"], aps["bias"],
          aps["lamv"], aps["gfin"], h1_dram, a_dram, out)
    r = run_bass_kernel_spmd(nc, [arrays], core_ids=[0])
    y = np.asarray(r.results[0]["out_0"])
    return y.transpose(1, 0, 2).reshape(1, T, D)
```
